# Optimizing a Trainium2 kernel written in Bass

```python
import math
import jax, jax.numpy as jnp
from jax import lax
import numpy as np

D_MODEL = 1024
BATCH = 1
SEQ = 512
DEPTH = 2

HEAD_DIM = 64
H_A = 8
KV_RANK = 128
H_IDX = 8
D_IDX = 64
TOPK_MAX = 256
H_B = 8
Q_BLOCK = 128
N_BUCKETS = 32
T5_MAX_DIST = 128
G_C = 8
CHUNK = 128
C_WIDTH = G_C * HEAD_DIM
G_D = 8
D_WIDTH = G_D * HEAD_DIM
CONV_W = 3
D_FF = 2816
N_EVEN = (DEPTH + 1) // 2
N_ODD = DEPTH // 2
ALPHA = (2.0 * DEPTH) ** 0.25
BETA = (8.0 * DEPTH) ** -0.25
LN_EPS = 1e-5
EVEN_WIDTHS = (H_A * HEAD_DIM, KV_RANK, H_IDX * D_IDX, D_IDX, H_IDX,
               H_B * HEAD_DIM, H_B * HEAD_DIM, H_B * HEAD_DIM, H_B)
ODD_WIDTHS = (C_WIDTH, C_WIDTH, D_WIDTH, D_WIDTH, D_WIDTH)
EVEN_PROJ = sum(EVEN_WIDTHS)
ODD_PROJ = sum(ODD_WIDTHS)
EVEN_MIX = H_A * HEAD_DIM + H_B * HEAD_DIM
ODD_MIX = C_WIDTH + D_WIDTH


def _split(h, widths):
    out, off = [], 0
    for w in widths:
        out.append(h[..., off:off + w])
        off += w
    return out

def layer_norm(x, g, b=None):
    xf = x.astype(jnp.float32)
    mu = jnp.mean(xf, axis=-1, keepdims=True)
    xc = xf - mu
    var = jnp.mean(xc * xc, axis=-1, keepdims=True)
    y = xc * lax.rsqrt(var + LN_EPS) * g.astype(jnp.float32)
    if b is not None:
        y = y + b.astype(jnp.float32)
    return y.astype(x.dtype)

def causal_dwconv(z, w):
    width, ch = w.shape
    return lax.conv_general_dilated(
        z, w[:, None, :].astype(z.dtype), window_strides=(1,),
        padding=[(width - 1, 0)], dimension_numbers=('NWC', 'WIO', 'NWC'),
        feature_group_count=ch)

def t5_bucket(dist):
    max_exact = N_BUCKETS // 2
    n = jnp.maximum(dist, 0)
    nf = jnp.maximum(n, 1).astype(jnp.float32)
    large = max_exact + (jnp.log(nf / max_exact) / math.log(T5_MAX_DIST / max_exact)
                         * (N_BUCKETS - max_exact)).astype(jnp.int32)
    large = jnp.minimum(large, N_BUCKETS - 1)
    return jnp.where(n < max_exact, n, large)

def to_blocks(a):
    return jnp.moveaxis(a.reshape(a.shape[0], -1, Q_BLOCK, *a.shape[2:]), 1, 0)

def from_blocks(a):
    a = jnp.moveaxis(a, 0, 1)
    return a.reshape(a.shape[0], -1, *a.shape[3:])

def even_mixer(x, w_in, w_uk, w_uv, b_f, w_o, rel_bias):
    bsz, seq, _ = x.shape
    k_sel = min(TOPK_MAX, seq // 4)
    n_blk = seq // Q_BLOCK
    h = x @ w_in
    q_a, c_kv, q_idx, k_idx, w_idx, q_b, k_b, v_b, f_in = _split(h, EVEN_WIDTHS)
    q_a = q_a.reshape(bsz, seq, H_A, HEAD_DIM)
    q_lat = jnp.einsum('bshd,hrd->bshr', q_a, w_uk) * (HEAD_DIM ** -0.5)
    q_idx = q_idx.reshape(bsz, seq, H_IDX, D_IDX) * (D_IDX ** -0.5)
    w_idx = w_idx * (H_IDX ** -0.5)
    q_b = q_b.reshape(bsz, seq, H_B, HEAD_DIM) * (HEAD_DIM ** -0.5)
    k_b = k_b.reshape(bsz, seq, H_B, HEAD_DIM)
    v_b = v_b.reshape(bsz, seq, H_B, HEAD_DIM)
    log_f = jax.nn.log_sigmoid(f_in.astype(jnp.float32) + b_f.astype(jnp.float32))
    cum_f = jnp.cumsum(log_f, axis=1)
    cum_f_keys = jnp.swapaxes(cum_f, 1, 2)

    key_pos = jnp.arange(seq)
    bidx = jnp.arange(bsz)[:, None, None]

    def block(args):
        i, ql, qi, wi, qb, fq = args
        q_pos = i * Q_BLOCK + jnp.arange(Q_BLOCK)
        causal = key_pos[None, :] <= q_pos[:, None]
        idx = jnp.einsum('bthd,bsd->bths', qi, k_idx)
        score = jnp.einsum('bth,bths->bts', wi, jax.nn.relu(idx)).astype(jnp.float32)
        score = jnp.where(causal[None], score, -jnp.inf)
        _, sel = lax.top_k(score, k_sel)
        valid = sel <= q_pos[None, :, None]
        c_sel = c_kv[bidx, sel]
        la = jnp.einsum('bthr,btkr->bhtk', ql, c_sel).astype(jnp.float32)
        bias = rel_bias[t5_bucket(q_pos[None, :, None] - sel)]
        la = la + jnp.moveaxis(bias, -1, 1).astype(jnp.float32)
        la = jnp.where(valid[:, None], la, -jnp.inf)
        pa = jax.nn.softmax(la, axis=-1).astype(c_sel.dtype)
        oa = jnp.einsum('bhtk,btkr->bthr', pa, c_sel)
        lb = jnp.einsum('bthd,bshd->bhts', qb, k_b).astype(jnp.float32)
        lb = lb + jnp.swapaxes(fq, 1, 2)[..., None] - cum_f_keys[:, :, None, :]
        lb = jnp.where(causal[None, None], lb, -jnp.inf)
        pb = jax.nn.softmax(lb, axis=-1).astype(v_b.dtype)
        ob = jnp.einsum('bhts,bshd->bthd', pb, v_b)
        return oa, ob

    oa, ob = lax.map(block, (jnp.arange(n_blk), to_blocks(q_lat), to_blocks(q_idx),
                             to_blocks(w_idx), to_blocks(q_b), to_blocks(cum_f)))
    o_a = jnp.einsum('bshr,hrd->bshd', from_blocks(oa), w_uv).reshape(bsz, seq, H_A * HEAD_DIM)
    o_b = from_blocks(ob).reshape(bsz, seq, H_B * HEAD_DIM)
    return jnp.concatenate([o_a, o_b], axis=-1) @ w_o

def odd_mixer(x, w_in, sgu_g, sgu_w, sgu_b, conv_w, w_o):
    bsz, seq, _ = x.shape
    h = x @ w_in
    u, v, g_b, g_c, z = _split(h, ODD_WIDTHS)
    u = jax.nn.gelu(u)
    v = layer_norm(jax.nn.gelu(v).reshape(bsz, seq, G_C, HEAD_DIM), sgu_g)
    v = v.reshape(bsz, seq // CHUNK, CHUNK, G_C, HEAD_DIM)
    mix = jnp.einsum('gts,bnsgd->bntgd', jnp.tril(sgu_w), v) + jnp.swapaxes(sgu_b, 0, 1)[:, :, None]
    o_c = u * mix.reshape(bsz, seq, C_WIDTH)
    o_d = g_b * causal_dwconv(g_c * z, conv_w)
    return jnp.concatenate([o_c, o_d], axis=-1) @ w_o

def conv_ffn(x, w_up, conv_w, w_down):
    h = causal_dwconv(x @ w_up, conv_w)
    g, v = jnp.split(h, 2, axis=-1)
    return (jax.nn.silu(g) * v) @ w_down

def first_inputs(seed: int = 0) -> dict:
    key = jax.random.key(seed)
    ks = jax.random.split(key, 18)

    def nrm(k, shape, scale):
        return jax.random.normal(k, shape, jnp.float32) * scale

    return {
        "x": nrm(ks[0], (BATCH, SEQ, D_MODEL), 1.0),
        "ln_g": 1.0 + nrm(ks[1], (DEPTH, 2, D_MODEL), 0.02),
        "ln_b": nrm(ks[2], (DEPTH, 2, D_MODEL), 0.02),
        "rel_bias": nrm(ks[3], (N_BUCKETS, H_A), 0.5),
        "ev_w_in": nrm(ks[4], (N_EVEN, D_MODEL, EVEN_PROJ), D_MODEL ** -0.5),
        "ev_w_uk": nrm(ks[5], (N_EVEN, H_A, KV_RANK, HEAD_DIM), KV_RANK ** -0.5),
        "ev_w_uv": nrm(ks[6], (N_EVEN, H_A, KV_RANK, HEAD_DIM), KV_RANK ** -0.5),
        "ev_b_f": jax.random.uniform(ks[7], (N_EVEN, H_B), jnp.float32, 1.0, 4.0),
        "ev_w_o": nrm(ks[8], (N_EVEN, EVEN_MIX, D_MODEL), BETA * EVEN_MIX ** -0.5),
        "od_w_in": nrm(ks[9], (N_ODD, D_MODEL, ODD_PROJ), D_MODEL ** -0.5),
        "od_sgu_g": 1.0 + nrm(ks[10], (N_ODD, G_C, HEAD_DIM), 0.02),
        "od_sgu_w": nrm(ks[11], (N_ODD, G_C, CHUNK, CHUNK), CHUNK ** -0.5),
        "od_sgu_b": 1.0 + nrm(ks[12], (N_ODD, G_C, CHUNK), 0.1),
        "od_conv_w": nrm(ks[13], (N_ODD, CONV_W, D_WIDTH), CONV_W ** -0.5),
        "od_w_o": nrm(ks[14], (N_ODD, ODD_MIX, D_MODEL), BETA * ODD_MIX ** -0.5),
        "ffn_w_up": nrm(ks[15], (DEPTH, D_MODEL, 2 * D_FF), D_MODEL ** -0.5),
        "ffn_conv_w": nrm(ks[16], (DEPTH, CONV_W, 2 * D_FF), CONV_W ** -0.5),
        "ffn_w_down": nrm(ks[17], (DEPTH, D_FF, D_MODEL), BETA * D_FF ** -0.5),
    }

def first_block(x, ln_g, ln_b, rel_bias, ev_w_in, ev_w_uk, ev_w_uv, ev_b_f, ev_w_o,
              od_w_in, od_sgu_g, od_sgu_w, od_sgu_b, od_conv_w, od_w_o,
              ffn_w_up, ffn_conv_w, ffn_w_down):
    for layer in range(DEPTH):
        j = layer // 2
        if layer % 2 == 0:
            m = even_mixer(x, ev_w_in[j], ev_w_uk[j], ev_w_uv[j], ev_b_f[j], ev_w_o[j], rel_bias)
        else:
            m = odd_mixer(x, od_w_in[j], od_sgu_g[j], od_sgu_w[j], od_sgu_b[j], od_conv_w[j], od_w_o[j])
        x = layer_norm(ALPHA * x + m, ln_g[layer, 0], ln_b[layer, 0])
        f = conv_ffn(x, ffn_w_up[layer], ffn_conv_w[layer], ffn_w_down[layer])
        x = layer_norm(ALPHA * x + f, ln_g[layer, 1], ln_b[layer, 1])
    return x


DEPTH_2 = 1

CTX_LEN = 256
GRID_W = 64
ATT_HEADS = 8
ATT_KV_HEADS = 2
ATT_GROUP = ATT_HEADS // ATT_KV_HEADS
ATT_HEAD_DIM = 64
ATT_WIDTH = ATT_HEADS * ATT_HEAD_DIM
ATT_KV_WIDTH = ATT_KV_HEADS * ATT_HEAD_DIM
AXIS_DIM = ATT_HEAD_DIM // 2
ROPE_THETA = 10000.0
HG_HEADS = 4
HG_HEAD_DIM = 128
HG_WIDTH = HG_HEADS * HG_HEAD_DIM
MIX_WIDTH = ATT_WIDTH + HG_WIDTH
CHUNK_2 = 64
D_FF_2 = ((8 * D_MODEL // 3 + 255) // 256) * 256
EPS = 1e-6
IN_SIZES = (ATT_WIDTH, ATT_KV_WIDTH, ATT_KV_WIDTH, HG_WIDTH, HG_WIDTH, HG_WIDTH, HG_WIDTH, HG_WIDTH)
IN_COLS = sum(IN_SIZES)
IN_SPLIT_IDX = tuple(int(v) for v in np.cumsum(IN_SIZES)[:-1])


def rmsnorm(x, g):
    xf = x.astype(jnp.float32)
    y = xf * lax.rsqrt(jnp.mean(xf * xf, axis=-1, keepdims=True) + EPS)
    return (y * g.astype(jnp.float32)).astype(x.dtype)

def modulate(h, shift, scale):
    return h * (1 + scale) + shift

def axial_rope_tables(n_tokens):
    n_rows = n_tokens // GRID_W
    row = jnp.repeat(jnp.arange(n_rows, dtype=jnp.float32), GRID_W)
    col = jnp.tile(jnp.arange(GRID_W, dtype=jnp.float32), n_rows)
    inv = ROPE_THETA ** (-jnp.arange(0, AXIS_DIM, 2, dtype=jnp.float32) / AXIS_DIM)
    ar = row[:, None] * inv
    ac = col[:, None] * inv
    ang = jnp.concatenate([ar, ar, ac, ac], axis=-1)
    return jnp.cos(ang), jnp.sin(ang)

def apply_rope(x, cos, sin):
    x4 = x.reshape(*x.shape[:-1], 2, 2, ATT_HEAD_DIM // 4)
    rot = jnp.stack([-x4[..., 1, :], x4[..., 0, :]], axis=-2).reshape(x.shape)
    return (x * cos[:, None, :] + rot * sin[:, None, :]).astype(x.dtype)

def latent_attention(qx, kx, vx, kc, vc):
    B, T = qx.shape[:2]
    nblk = T // Q_BLOCK
    keys = jnp.concatenate([kc, kx], axis=1)
    vals = jnp.concatenate([vc, vx], axis=1)
    qb = qx.reshape(B, nblk, Q_BLOCK, ATT_KV_HEADS, ATT_GROUP, ATT_HEAD_DIM).transpose(1, 0, 2, 3, 4, 5)
    scale = ATT_HEAD_DIM ** -0.5

    def block(q):
        s = jnp.einsum('bqkgd,bnkd->bkgqn', q, keys).astype(jnp.float32) * scale
        p = jax.nn.softmax(s, axis=-1)
        return jnp.einsum('bkgqn,bnkd->bqkgd', p.astype(vals.dtype), vals)

    o = lax.map(block, qb)
    return o.transpose(1, 0, 2, 3, 4, 5).reshape(B, T, ATT_WIDTH)

def context_attention(qc, kc, vc):
    B, L = qc.shape[:2]
    q = qc.reshape(B, L, ATT_KV_HEADS, ATT_GROUP, ATT_HEAD_DIM)
    s = jnp.einsum('bqkgd,bnkd->bkgqn', q, kc).astype(jnp.float32) * (ATT_HEAD_DIM ** -0.5)
    p = jax.nn.softmax(s, axis=-1)
    o = jnp.einsum('bkgqn,bnkd->bqkgd', p.astype(vc.dtype), vc)
    return o.reshape(B, L, ATT_WIDTH)

def gla_chunked(q, k, v, logf, s0):
    B, T, H, DK = q.shape
    n = T // CHUNK_2

    def to_chunks(a):
        return a.reshape(B, n, CHUNK_2, H, a.shape[-1]).transpose(1, 0, 3, 2, 4)

    mask = jnp.tril(jnp.ones((CHUNK_2, CHUNK_2), dtype=bool))[:, :, None]

    def step(S, inp):
        qc, kc, vc, lf = inp
        b = jnp.cumsum(lf, axis=-2)
        diff = b[:, :, :, None, :] - b[:, :, None, :, :]
        decay = jnp.where(mask, jnp.exp(jnp.minimum(diff, 0.0)), 0.0)
        A = jnp.einsum('bhtk,bhsk,bhtsk->bhts', qc, kc, decay)
        o = jnp.einsum('bhts,bhsv->bhtv', A, vc) + jnp.einsum('bhtk,bhkv->bhtv', qc * jnp.exp(b), S)
        b_last = b[:, :, -1, :]
        S_new = jnp.exp(b_last)[..., None] * S + jnp.einsum(
            'bhsk,bhsv->bhkv', kc * jnp.exp(b_last[:, :, None, :] - b), vc)
        return S_new, o

    S, o = lax.scan(step, s0, (to_chunks(q), to_chunks(k), to_chunks(v), to_chunks(logf)))
    return o.transpose(1, 0, 3, 2, 4).reshape(B, T, H, v.shape[-1]), S

def hgrn2_prep(q, i, f, lb_d):
    B, T = q.shape[:2]
    fg = lb_d + (1.0 - lb_d) * jax.nn.sigmoid(f.astype(jnp.float32))
    sh = lambda a: a.reshape(B, T, HG_HEADS, HG_HEAD_DIM)
    qh = sh(jax.nn.silu(q.astype(jnp.float32)) * (HG_HEAD_DIM ** -0.5))
    return qh, sh(1.0 - fg), sh(i.astype(jnp.float32)), sh(jnp.log(fg))

def hgrn2_bidirectional(px, pc, lb_l, gain):
    qx, ix, ffx, fbx, gx = px
    qc, ic, ffc, fbc, gc = pc
    B = qx.shape[0]
    s0 = jnp.zeros((B, HG_HEADS, HG_HEAD_DIM, HG_HEAD_DIM), jnp.float32)
    flip = lambda a: a[:, ::-1]
    oc_f, sc_f = gla_chunked(*hgrn2_prep(qc, ic, ffc, lb_l[0]), s0)
    ox_f, _ = gla_chunked(*hgrn2_prep(qx, ix, ffx, lb_l[0]), sc_f)
    oc_b, sc_b = gla_chunked(*map(flip, hgrn2_prep(qc, ic, fbc, lb_l[1])), s0)
    ox_b, _ = gla_chunked(*map(flip, hgrn2_prep(qx, ix, fbx, lb_l[1])), sc_b)

    def readout(o_f, o_b, g):
        Bn, T = g.shape[:2]
        o = rmsnorm(o_f + flip(o_b), gain).reshape(Bn, T, HG_WIDTH)
        return (o * jax.nn.silu(g.astype(jnp.float32))).astype(g.dtype)

    return readout(ox_f, ox_b, gx), readout(oc_f, oc_b, gc)

def swiglu(h, w_gu, w_down):
    a, b = jnp.split(h @ w_gu, 2, axis=-1)
    return (jax.nn.silu(a) * b) @ w_down

def second_inputs(seed: int = 0) -> dict:
    key = jax.random.key(seed)
    ks = jax.random.split(key, 17)
    nrm = lambda k, shape, s: jax.random.normal(k, shape, jnp.float32) * s
    return {
        "x": nrm(ks[0], (BATCH, SEQ, D_MODEL), 1.0),
        "c": nrm(ks[1], (BATCH, D_MODEL), 1.0),
        "ctx": nrm(ks[2], (BATCH, CTX_LEN, D_MODEL), 1.0),
        "c_ctx": nrm(ks[3], (D_MODEL,), 1.0),
        "w_mod": nrm(ks[4], (DEPTH_2, D_MODEL, 6 * D_MODEL), 0.5 * D_MODEL ** -0.5),
        "b_mod": nrm(ks[5], (DEPTH_2, 6 * D_MODEL), 0.02),
        "g_norm1": 1.0 + nrm(ks[6], (DEPTH_2, D_MODEL), 0.02),
        "w_in": nrm(ks[7], (DEPTH_2, D_MODEL, IN_COLS), D_MODEL ** -0.5),
        "g_q": 1.0 + nrm(ks[8], (DEPTH_2, ATT_HEAD_DIM), 0.02),
        "g_k": 1.0 + nrm(ks[9], (DEPTH_2, ATT_HEAD_DIM), 0.02),
        "lb_raw": nrm(ks[10], (DEPTH_2 + 1, 2, HG_WIDTH), 0.5),
        "g_hg": 1.0 + nrm(ks[11], (DEPTH_2, HG_HEAD_DIM), 0.02),
        "w_out": nrm(ks[12], (DEPTH_2, MIX_WIDTH, D_MODEL), MIX_WIDTH ** -0.5),
        "g_norm2": 1.0 + nrm(ks[13], (DEPTH_2, D_MODEL), 0.02),
        "w_gu": nrm(ks[14], (DEPTH_2, D_MODEL, 2 * D_FF_2), D_MODEL ** -0.5),
        "w_down": nrm(ks[15], (DEPTH_2, D_FF_2, D_MODEL), D_FF_2 ** -0.5),
        "g_final": 1.0 + nrm(ks[16], (D_MODEL,), 0.02),
    }

def second_block(x, c, ctx, c_ctx, w_mod, b_mod, g_norm1, w_in, g_q, g_k, lb_raw, g_hg, w_out,
              g_norm2, w_gu, w_down, g_final):
    B, T = x.shape[:2]
    cos, sin = axial_rope_tables(T)
    lb_all = jnp.cumsum(jax.nn.softmax(lb_raw.astype(jnp.float32), axis=0), axis=0)
    heads = lambda a, h, d: a.reshape(a.shape[0], a.shape[1], h, d)
    for l in range(DEPTH_2):
        last = l == DEPTH_2 - 1
        mx = [m[:, None, :] for m in jnp.split(jax.nn.silu(c) @ w_mod[l] + b_mod[l], 6, axis=-1)]
        mc = jnp.split(jax.nn.silu(c_ctx) @ w_mod[l] + b_mod[l], 6, axis=-1)
        hx = modulate(rmsnorm(x, g_norm1[l]), mx[0], mx[1])
        hc = modulate(rmsnorm(ctx, g_norm1[l]), mc[0], mc[1])
        px = jnp.split(hx @ w_in[l], IN_SPLIT_IDX, axis=-1)
        pc = jnp.split(hc @ w_in[l], IN_SPLIT_IDX, axis=-1)
        qx = apply_rope(rmsnorm(heads(px[0], ATT_HEADS, ATT_HEAD_DIM), g_q[l]), cos, sin)
        kx = apply_rope(rmsnorm(heads(px[1], ATT_KV_HEADS, ATT_HEAD_DIM), g_k[l]), cos, sin)
        vx = heads(px[2], ATT_KV_HEADS, ATT_HEAD_DIM)
        kc = rmsnorm(heads(pc[1], ATT_KV_HEADS, ATT_HEAD_DIM), g_k[l])
        vc = heads(pc[2], ATT_KV_HEADS, ATT_HEAD_DIM)
        att_x = latent_attention(qx, kx, vx, kc, vc)
        hg_x, hg_c = hgrn2_bidirectional(px[3:], pc[3:], lb_all[l], g_hg[l])
        x = x + mx[2] * (jnp.concatenate([att_x, hg_x], axis=-1) @ w_out[l])
        x = x + mx[5] * swiglu(modulate(rmsnorm(x, g_norm2[l]), mx[3], mx[4]), w_gu[l], w_down[l])
        if not last:
            qc = rmsnorm(heads(pc[0], ATT_HEADS, ATT_HEAD_DIM), g_q[l])
            att_c = context_attention(qc, kc, vc)
            ctx = ctx + mc[2] * (jnp.concatenate([att_c, hg_c], axis=-1) @ w_out[l])
            ctx = ctx + mc[5] * swiglu(modulate(rmsnorm(ctx, g_norm2[l]), mc[3], mc[4]), w_gu[l], w_down[l])
    return rmsnorm(x, g_final)


def setup_inputs(seed=0):
    out = dict(first_inputs(seed))
    for name, value in second_inputs(seed + 1).items():
        if name != "x":
            out[name + "_2"] = value
    return out


def reference(
    x, ln_g, ln_b, rel_bias, ev_w_in, ev_w_uk, ev_w_uv, ev_b_f, ev_w_o, od_w_in, od_sgu_g,
    od_sgu_w, od_sgu_b, od_conv_w, od_w_o, ffn_w_up, ffn_conv_w, ffn_w_down, c_2, ctx_2,
    c_ctx_2, w_mod_2, b_mod_2, g_norm1_2, w_in_2, g_q_2, g_k_2, lb_raw_2, g_hg_2, w_out_2,
    g_norm2_2, w_gu_2, w_down_2, g_final_2,
):
    x = first_block(
        x, ln_g, ln_b, rel_bias, ev_w_in, ev_w_uk, ev_w_uv, ev_b_f, ev_w_o, od_w_in, od_sgu_g,
        od_sgu_w, od_sgu_b, od_conv_w, od_w_o, ffn_w_up, ffn_conv_w, ffn_w_down,
    )
    return second_block(
        x, c_2, ctx_2, c_ctx_2, w_mod_2, b_mod_2, g_norm1_2, w_in_2, g_q_2, g_k_2, lb_raw_2,
        g_hg_2, w_out_2, g_norm2_2, w_gu_2, w_down_2, g_final_2,
    )


_drawn_inputs = setup_inputs


def setup_inputs(seed=0):
    import zlib

    import numpy as np

    out = dict(_drawn_inputs(seed))
    spreads = {}
    factors = {'rel_bias': 3.224,
     'od_sgu_g': 8.0,
     'od_sgu_b': 3.558,
     'ctx_2': 6.271,
     'c_ctx_2': 2.825,
     'b_mod_2': 2.71,
     'g_norm1_2': 8.0,
     'g_q_2': 8.0,
     'g_k_2': 8.0,
     'lb_raw_2': 8.0,
     'g_hg_2': 8.0,
     'g_norm2_2': 8.0,
     'g_final_2': 2.732}
    for name, (base, spread) in spreads.items():
        noise = np.random.default_rng([zlib.crc32(name.encode()), seed]).standard_normal(out[name].shape)
        drawn = base * np.exp(spread * noise) if base else spread * noise
        out[name] = __import__('jax').numpy.asarray(drawn.astype(out[name].dtype))
    for name, factor in factors.items():
        out[name] = (out[name] * factor).astype(out[name].dtype)
    return out
```

```python
import math
from contextlib import ExitStack

import concourse.bass as bass
import numpy as np
from concourse import mybir

F32 = mybir.dt.float32
F32R = mybir.dt.float32r
U8 = mybir.dt.uint8
ALU = mybir.AluOpType
ACT = mybir.ActivationFunctionType
AX = mybir.AxisListType

P = 128
D = 1024
KD = D // P
T = 512
NB = T // P
LC = 256
HEADS, HD = 8, 64
D_IDX = 64
TOPK = min(256, T // 4)
FF = 2816
NFF = FF // P
N_BUCKETS, T5_MAX = 32, 128
ALPHA = (2.0 * 2) ** 0.25
LN_EPS, RMS_EPS = 1e-5, 1e-6
HG = 4
GRID_W, ROPE_THETA = 64, 10000.0
GATE_FLOOR = 2.0 ** -64
HG_SCALE = 0.25
NEG = -1.0e30
MARK = -3.0e38
OUT_OF_REACH = -2.0e38
SKEW = 3 * P - 1

EV_QA, EV_QI, EV_QB, EV_KB, EV_VB, EV_CKV, EV_KI, EV_MISC, EV_N = 0, 4, 8, 12, 16, 20, 21, 22, 23
W_IDX_ROW = 32
OD_U, OD_V, OD_GB, OD_GC, OD_Z, OD_N = 0, 4, 8, 12, 16, 20
SB_Q, SB_HQ, SB_HG, SB_K, SB_V, SB_I, SB_FF, SB_FB, SB_N = 0, 4, 8, 12, 13, 14, 18, 22, 26
SB_CTX = SB_K

RAW, SPLIT = 4, 2
CHUNK = 11 * P


class Weights:

    def __init__(self, signals, dram, kt, before):
        self.dram, self.n, self.kt, self.cols = dram, dram.shape[0], kt, kt * P
        self.before, self.next = before, None
        self.loaded, self.high, self.low, self.used = signals
        self.c0 = before.c0 + before.n if before else 0
        self.l0 = [before.l0[s] + len(range(s, before.n, RAW)) if before else 0 for s in range(RAW)]
        self.freed = [before.c0 + max(range(s, before.n, SPLIT)) + 1 if before else 0 for s in range(SPLIT)]


def after(count, number):
    return count + number if number else count


class Steps:

    def __init__(self, sem):
        self.sem, self.n = sem, 0

    def mark(self, ins):
        ins.then_inc(self.sem, 1)
        self.n += 1
        return self.n


def build(nc, A, out):
    with ExitStack() as ctx:
        def sem(name):
            return ctx.enter_context(nc.semaphore(name))

        place = {"at": (nc.sbuf_base + 31) // 32 * 32}

        def sb(name, shape, dt=F32, at=None):
            size = int(np.prod(shape[1:])) * (1 if dt == U8 else 4)
            size = (size + 31) // 32 * 32
            off = place["at"] if at is None else at
            if at is None:
                place["at"] += size
            assert off + size <= nc.sbuf_usable_end, (name, off + size)
            return nc.alloc_sbuf_tensor_at(name, shape, dt, offset=off), off + size

        def keep(name, shape, dt=F32):
            return sb(name, shape, dt)[0]
        raw_at = place["at"]
        raw = keep("w_raw", [P, RAW, CHUNK])
        split_at = place["at"]
        w_hi = keep("w_hi", [P, SPLIT, CHUNK], F32R)
        w_lo = keep("w_lo", [P, SPLIT, CHUNK], F32R)
        split_end = place["at"]
        xT = keep("xT", [P, KD, T])
        xH = keep("xH", [P, KD, T], F32R)
        xL = keep("xL", [P, KD, T], F32R)
        ident = keep("ident", [P, P])
        mean_of = keep("mean_of", [P, P])
        cols = keep("cols", [P, A["cols"].shape[1]])
        modT = keep("modT", [P, 48, 2])
        gmod = keep("gmod", [P, 3, KD])
        warm = keep("warm", [P, 3])
        ARENA = place["at"]

        psum = ctx.enter_context(nc.psum_tensor("psum", [P, 8 * T], F32))
        bank = [psum[:, b * T:(b + 1) * T] for b in range(8)]

        signals = ([sem(f"w_loaded{s}") for s in range(RAW)], sem("w_high"), sem("w_low"), sem("w_used"))
        W, before = {}, None
        for name, kt in (("ev_in", KD), ("ev_out", KD), ("up0", KD), ("down0", NFF // 2),
                         ("od_in", KD), ("od_out", KD), ("up1", KD), ("down1", NFF // 2),
                         ("sb_in", KD), ("sb_out", KD), ("up2", KD), ("down2", NFF // 2)):
            W[name] = Weights(signals, A[name], kt, before)
            if before:
                before.next = W[name]
            before = W[name]

        def load_chunk(sp, w, s, c):
            sp.dma_start(raw[:, s, 0:w.cols], w.dram[c]).then_inc(w.loaded[s], 16)

        def prefetch(sp, w):
            for s in range(RAW):
                if w.before:
                    sp.wait_ge(w.low, w.before.c0 + max(range(s, w.before.n, RAW)) + 1)
                load_chunk(sp, w, s, s)

        def stream_in(sp, w):
            full = w.n // RAW
            with sp.Fori(1, full) as i:
                for s in range(RAW):
                    sp.wait_ge(w.low, i * RAW + (w.c0 + s - RAW + 1))
                    load_chunk(sp, w, s, i * RAW + s)
            for c in range(full * RAW, w.n):
                sp.wait_ge(w.low, w.c0 + c - RAW + 1)
                load_chunk(sp, w, c % RAW, c)

        def split_high(act, w, i, j):
            s = j % RAW
            act.wait_ge(w.loaded[s], (i + j // RAW) * 16 + 16 * (w.l0[s] + 1))
            if not (isinstance(i, int) and i * RAW + j < SPLIT):
                act.wait_ge(w.used, i * RAW + (w.c0 + j - SPLIT + 1))
            elif w.before:
                act.wait_ge(w.used, w.freed[j])
            nc.scalar.activation(w_hi[:, s % SPLIT, 0:w.cols], raw[:, s, 0:w.cols], ACT.Copy).then_inc(w.high, 1)

        def split_low(dve, w, i, j):
            s = j % RAW
            dve.wait_ge(w.high, i * RAW + (w.c0 + j + 1))
            nc.vector.tensor_tensor(w_lo[:, s % SPLIT, 0:w.cols], raw[:, s, 0:w.cols],
                                    w_hi[:, s % SPLIT, 0:w.cols].bitcast(F32), ALU.subtract).then_inc(w.low, 1)

        def chunks(eng, n, body, first=0):
            full = (n - SPLIT) // RAW
            if full > 1:
                with eng.Fori(first // RAW, full) as i:
                    for j in range(RAW):
                        body(i, j, True)
            else:
                full = 0
            for c in range(full * RAW, n):
                body(c // RAW, c % RAW, c + SPLIT < n)

        def tiles(eng, n, body, first=0):
            full = n // RAW
            with eng.Fori(first // RAW, full) as i:
                for j in range(RAW):
                    body(i, j)
            for c in range(full * RAW, n):
                body(c // RAW, c % RAW)

        def products(pe, w, slot, right, acc, k0=0, first=True, last=True, x_ready=None):
            h, l = right
            for k in range(w.kt):
                if x_ready is not None:
                    pe.wait_ge(x_ready[0], x_ready[1] + k + 1)
                cut = slice(k * P, (k + 1) * P)
                for n, (a, b) in enumerate(((w_hi, h), (w_hi, l), (w_lo, h))):
                    mm = nc.tensor.matmul(acc, a[:, slot % SPLIT, cut], b[:, k0 + k, :],
                                          start=first and k == 0 and n == 0, stop=last and k == w.kt - 1 and n == 2)
            return mm

        x_ready = sem("x_ready")
        X = (xH, xL)

        acc_free = [sem("acc_free0"), sem("acc_free1")]
        freed = [0, 0]

        class Part:

            def sync(self, sp):
                pass

            scalar = vector = tensor = gpsimd = sync

        class Stage(Part):

            def __init__(self, w, right, per=1, x_base=None, emptied_by=None):
                self.w, self.right, self.per, self.x_base = w, right, per, x_base
                self.f0 = list(freed)
                nt = w.n // per
                for b in range(2):
                    freed[b] += len(range(b, nt, 2))

            chain = True

            def sync(self, sp):
                stream_in(sp, self.w)
                if self.chain and self.w.next:
                    prefetch(sp, self.w.next)

            def bank_of(self, j):
                return (j // self.per) % 2

            def free_at(self, i, j):
                return i * (RAW // self.per // 2) + (self.f0[self.bank_of(j)] + j // self.per // 2 + 1)

            def emptied(self, ins, j):
                ins.then_inc(acc_free[self.bank_of(j)], 1)

            def finished(self, eng, i, j):
                eng.wait_ge(self.w.used, i * RAW + (self.w.c0 + j + 1))

            def tensor(self, pe):
                w = self.w

                def tile(i, j):
                    b, part = self.bank_of(j), j % self.per
                    if part == 0:
                        pe.wait_ge(acc_free[b], self.free_at(i, j))
                    pe.wait_ge(w.low, i * RAW + (w.c0 + j + 1))
                    products(pe, w, j, self.right, bank[b][:, :], k0=part * w.kt, first=part == 0,
                             last=part == self.per - 1,
                             x_ready=(x_ready, self.x_base) if j == 0 and self.x_base is not None else None)\
                        .then_inc(w.used, 1)
                tiles(pe, w.n, tile)

            def first_high(self, act):
                for j in range(SPLIT):
                    split_high(act, self.w, 0, j)

            def first_low(self, dve):
                for j in range(SPLIT):
                    split_low(dve, self.w, 0, j)

        class Project(Stage):

            def __init__(self, w, hT, x_base):
                super().__init__(w, X, 1, x_base)
                self.hT = hT

            def scalar(self, act):
                self.first_high(act)

                def tile(i, j, ahead):
                    self.finished(act, i, j)
                    self.emptied(nc.scalar.activation(self.hT[:, i * RAW + j, :], bank[j % 2][:, :], ACT.Copy), j)
                    if ahead:
                        split_high(act, self.w, i, j + SPLIT)
                chunks(act, self.w.n, tile)

            def vector(self, dve):
                self.first_low(dve)
                chunks(dve, self.w.n, lambda i, j, ahead: split_low(dve, self.w, i, j + SPLIT) if ahead else None)

        at = ARENA
        hT, at = sb("ev_hT", [P, EV_N, T], at=at)
        near, at = sb("near_bias", [P, HEADS, 2 * P], at=at)
        far, at = sb("far_bias", [P, HEADS], at=at)
        csil, at = sb("c_silu", [P, D], at=at)
        ATT = at
        relb, at = sb("relb", [N_BUCKETS, HEADS], at=at)
        relrep, at = sb("relrep", [N_BUCKETS, HEADS, P], at=at)
        onehot, at = sb("onehot", [N_BUCKETS, SKEW], at=at)
        brow, at = sb("brow", [P, HEADS, SKEW], at=at)
        cctx, at = sb("cctx_silu", [P, D], at=at)
        product, at = sb("mod_product", [P, D], at=at)
        mod_part, at = sb("mod_part", [P, RAW, 2], at=at)
        mod_raw, at = sb("mod_raw", [P, RAW, D], at=at)
        skew = nc.dram_tensor("skew", (HEADS * P * SKEW,), F32, kind="Internal").ap()

        s_x = [sem(f"x_in{k}") for k in range(KD // 2)]
        s_par = sem("params_in")
        s_rel = sem("rel_in")
        s_xh, s_rep, s_brow, s_bmm, s_skew, s_near, s_cs = map(sem, (
            "x_high", "rel_repeated", "bias_rows_out", "bias_rows", "skew_written", "near_in", "c_silu"))
        ev = Project(W["ev_in"], hT, 0)
        ev.chain = False
        mod_n = A["mod"].shape[0]
        mod_first = 20
        mod_ctx = 2 * KD
        mod_in = [sem(f"mod_in{s}") for s in range(RAW)]
        mod_rest = [sem(f"mod_rest{s}") for s in range(RAW)]
        mod_used, mod_ctx_done, mod_ready = sem("mod_used"), sem("mod_ctx_done"), sem("mod_ready")

        def load_mod(eng, ring, s, c, done):
            eng.dma_start(ring[:, s, 0:D], A["mod"][c]).then_inc(done[s], 16)

        def row_sums(w, silu, column, product):
            return nc.vector.tensor_tensor_reduce(out=product, in0=w, in1=silu[:, :], scale=1.0, scalar=0.0, op0=ALU.mult,
                                                  op1=ALU.add, accum_out=column)

        def modulation(dve, i, j, vectors):
            dve.wait_ge(mod_in[j], i * 16 + 16)
            if j == 0:
                dve.wait_ge(mod_ready, i + 1)
            w = mod_raw[:, j, :]
            if vectors == 2:
                if j:
                    dve.wait_ge(mod_used, i * RAW + j)
                row_sums(w, cctx, mod_part[:, j, 1:2], product[:, :]).then_inc(mod_ctx_done, 1)
                dve.wait_ge(mod_ctx_done, i * RAW + (j + 1))
            row_sums(w, csil, mod_part[:, j, 0:1], w).then_inc(mod_used, 1)
            if j == RAW - 1:
                dve.wait_ge(mod_used, i * RAW + RAW)
                nc.vector.tensor_copy(modT[:, :, :].rearrange("p (i j) v -> p i j v", j=RAW)[:, i, :, 0:vectors], mod_part[:, :, 0:vectors]).then_inc(mod_ready, 1)

        with nc.Block() as block:
            @block.sync
            def _(sp):
                for k in range(KD // 2):
                    sp.dma_start(xT[:, 2 * k:2 * k + 2, :], A["xT"][:, 2 * k:2 * k + 2, :]).then_inc(s_x[k], 16)
                prefetch(sp, W["ev_in"])
                ev.sync(sp)
                sp.wait_ge(s_brow, HEADS)
                sp.dma_start(skew.rearrange("(h p d) -> p h d", h=HEADS, p=P), brow[:, :, :]).then_inc(s_skew, 16)
                sp.wait_ge(s_skew, 16)
                for h in range(HEADS):
                    a = h * P * SKEW + P - 1
                    src = skew[a:a + P * (SKEW - 1)].rearrange("(p d) -> p d", p=P)[:, 0:2 * P]
                    sp.dma_start(near[:, h, :], src).then_inc(s_near, 16)
                sp.wait_ge(s_near, 16 * HEADS)

            @block.gpsimd
            def _(pool):
                for s in range(RAW):
                    load_mod(pool, mod_raw, s, s, mod_in)
                with pool.Fori(1, mod_first // RAW) as i:
                    for s in range(RAW):
                        pool.wait_ge(mod_used, i * RAW + (s - RAW + 1))
                        load_mod(pool, mod_raw, s, i * RAW + s, mod_in)

            @block.scalar
            def _(act):
                for b in range(2):
                    act.sem_inc(acc_free[b], 1)
                act.dma_start(ident[:, :], A["ident"]).then_inc(s_par, 16)
                act.dma_start(mean_of[:, :], A["mean_of"]).then_inc(s_par, 16)
                act.dma_start(cols[:, :], A["cols"]).then_inc(s_par, 16)
                act.dma_start(csil[:, :], A["c_rows"][0]).then_inc(s_rel, 16)
                act.dma_start(cctx[:, :], A["c_rows"][1]).then_inc(s_rel, 16)
                act.dma_start(relb[:, :], A["rel_bias"]).then_inc(s_rel, 16)
                act.dma_start(onehot[:, :], A["onehot"]).then_inc(s_rel, 16)
                for k in range(KD):
                    act.wait_ge(s_x[k // 2], 16)
                    nc.scalar.activation(xH[:, k, :], xT[:, k, :], ACT.Copy).then_inc(s_xh, 1)
                act.wait_ge(s_rel, 64)
                nc.scalar.activation(csil[:, :], csil[:, :], ACT.Silu).then_inc(s_cs, 1)
                nc.scalar.activation(cctx[:, :], cctx[:, :], ACT.Silu).then_inc(s_cs, 1)
                for h in range(HEADS):
                    act.wait_ge(s_bmm, h + 1)
                    nc.scalar.activation(brow[:, h, :], bank[2 + h % 2][:, 0:SKEW], ACT.Copy).then_inc(s_brow, 1)
                act.wait_ge(s_brow, HEADS)
                nc.scalar.activation(far[:, :], brow[:, :, 0], ACT.Copy).then_inc(s_cs, 1)
                ev.scalar(act)

            @block.vector
            def _(dve):
                for k in range(KD):
                    dve.wait_ge(s_xh, k + 1)
                    nc.vector.tensor_tensor(xL[:, k, :], xT[:, k, :], xH[:, k, :].bitcast(F32),
                                            ALU.subtract).then_inc(x_ready, 1)
                dve.wait_ge(s_rel, 64)
                nc.vector.tensor_copy(relrep[:, :, :], relb[:, :].unsqueeze(2).to_broadcast([N_BUCKETS, HEADS, P]))\
                    .then_inc(s_rep, 1)
                nc.vector.memset(mod_part[:, :, :], 0.0).then_inc(mod_ready, 1)
                dve.wait_ge(s_cs, 2)
                ev.first_low(dve)
                w = W["ev_in"]

                def tile(i, j, vectors):
                    split_low(dve, w, i, j + SPLIT)
                    modulation(dve, i, j, vectors)
                with dve.Fori(0, mod_ctx // RAW) as i:
                    for j in range(RAW):
                        tile(i, j, 2)
                with dve.Fori(mod_ctx // RAW, mod_first // RAW) as i:
                    for j in range(RAW):
                        tile(i, j, 1)
                for c in range(mod_first, w.n - SPLIT):
                    split_low(dve, w, c // RAW, c % RAW + SPLIT)

            @block.tensor
            def _(pe):
                pe.wait_ge(s_rep, 1)
                for h in range(HEADS):
                    if h >= 2:
                        pe.wait_ge(s_brow, h - 1)
                    nc.tensor.matmul(bank[2 + h % 2][:, 0:SKEW], relrep[:, h, :], onehot[:, :],
                                     start=True, stop=True).then_inc(s_bmm, 1)
                ev.tensor(pe)

        RING = 5
        at = ATT
        w_uk, at = sb("w_uk", [P, 4, P], at=at)
        w_uv, at = sb("w_uv", [P, HEADS, HD], at=at)
        c_tm, at = sb("c_tm", [P, NB, P], at=at)
        v_tm, at = sb("v_tm", [P, NB, HEADS * HD], at=at)
        wtm, at = sb("wtm", [P, NB, HEADS], at=at)
        fq8, at = sb("fq8", [P, NB, HEADS], at=at)
        cumf, at = sb("cumf", [HEADS, T], at=at)
        causal, at = sb("causal", [P, P], at=at)
        ncum8, at = sb("ncum8", [P, HEADS, T], at=at)
        score, at = sb("score", [P, T], at=at)
        pTa, at = sb("pTa", [P, NB, 4, P], at=at)
        pTb, at = sb("pTb", [P, 2, NB, P], at=at)
        Xa, at = sb("addend", [P, 3, T], at=at)
        at3 = ARENA + EV_VB * T * 4
        oaT, at3 = sb("oaT", [P, HEADS, P], at=at3)
        stat, at3 = sb("stat", [P, 3, 16 * NB], at=at3)
        top8, at3 = sb("top8", [P, 8], at=at3)
        at2 = split_at
        lf, _ = sb("log_f", [HEADS, 3, T], at=at2)
        tl, at2 = sb("logits", [P, RING, T], at=at2)
        rbuf, at2 = sb("rbuf", [P, 2, T], at=at2)
        qlT, at2 = sb("qlT", [P, 2, HEADS, P], at=at2)
        mneg, at3 = sb("mneg", [P, T], at=at3)
        assert at2 <= split_end and at3 <= ARENA + EV_CKV * T * 4
        UNITS = 16

        a = {n: sem("att_" + n) for n in (
            "par", "turned", "turned_out", "lsig", "cumf", "spread", "spread_out", "causal", "col", "col_out",
            "logits", "relu", "score", "masked", "topk", "mneg", "addend", "ttr", "exp", "recip", "norm",
            "prob_t", "prob_out", "pv_b", "o_b_hi", "o_b_lo", "b5", "b5_out", "o_a_lo", "mod_evac", "zero")}

        TURN, OUT, PV = 3, 4, 5
        jobs = []
        for i in range(NB):
            for k in range(2 * HEADS):
                jobs.append(("b" if k < HEADS else "a", i, k % HEADS))
                if k < HEADS and i + 1 < NB:
                    jobs.append(("s", i + 1, k))
        nth = {job: n for n, job in enumerate(jobs)}

        def outputs(i, what):
            n = 2 + 5 * i + (1 if what[0] == "q" else 3 if i + 1 < NB else 1) + what[1]
            return n if what[0] != "o" else n + 2

        def unit(i, k):
            return UNITS * i + k

        def job_of(i, k):
            return ("b", i, k) if k < HEADS else ("a", i, k - HEADS)

        def rows(h):
            return slice((h % 2) * HD, (h % 2) * HD + HD)

        def blk(i):
            return slice(i * P, (i + 1) * P)

        with nc.Block() as block:
            @block.sync
            def _(sp):
                sp.dma_start(w_uk[:, :, :], A["w_uk"]).then_inc(a["par"], 16)
                sp.dma_start(w_uv[:, :, :], A["w_uv"]).then_inc(a["par"], 16)
                for s in range(RAW):
                    load_mod(sp, raw, s, mod_first + s, mod_rest)
                with sp.Fori(mod_first // RAW + 1, mod_n // RAW) as i:
                    for s in range(RAW):
                        sp.wait_ge(mod_used, i * RAW + (s - RAW + 1))
                        load_mod(sp, raw, s, i * RAW + s, mod_rest)
                sp.wait_ge(mod_used, mod_n)
                prefetch(sp, W["ev_out"])

            @block.gpsimd
            def _(pool):
                nc.gpsimd.memset(causal[:, :], 0.0).then_inc(a["zero"], 1)
                pool.wait_ge(a["zero"], 1)
                nc.gpsimd.affine_select(out=causal[:, :], in_=causal[:, :], compare_op=ALU.is_ge, fill=NEG, base=0,
                                        pattern=[[-1, P]], channel_multiplier=1).then_inc(a["causal"], 1)
                pool.wait_ge(a["col_out"], 1)
                pool.wait_ge(a["spread_out"], HEADS)
                for i in range(NB):
                    w = (i + 1) * P
                    for k in range(UNITS):
                        u, h = unit(i, k), k % HEADS
                        if u >= 3:
                            pool.wait_ge(a["ttr"], u - 2)
                        X = Xa[:, u % 3, :]
                        if k < HEADS:
                            nc.gpsimd.tensor_scalar(X[:, 0:w], ncum8[:, h, 0:w], 1.0, fq8[:, i, h:h + 1],
                                                    ALU.mult, ALU.add).then_inc(a["zero"], 1)
                            pool.wait_ge(a["zero"], 2 + HEADS * i + h)
                            nc.gpsimd.affine_select(out=X[:, blk(i)], in_=X[:, blk(i)], compare_op=ALU.is_ge, fill=NEG,
                                                    base=0, pattern=[[-1, P]], channel_multiplier=1).then_inc(a["addend"], 1)
                        else:
                            if k == HEADS:
                                pool.wait_ge(a["mneg"], i + 1)
                            n = min(w, 2 * P)
                            if w > n:
                                nc.gpsimd.tensor_scalar(X[:, 0:w - n], mneg[:, 0:w - n], 1.0, far[:, h:h + 1],
                                                        ALU.mult, ALU.add)
                            nc.gpsimd.tensor_tensor(X[:, w - n:w], mneg[:, w - n:w], near[:, h, 2 * P - n:2 * P],
                                                    ALU.add).then_inc(a["addend"], 1)
                        if k == HEADS + 2 and i + 1 < NB:
                            pool.wait_ge(a["score"], HEADS * (i + 1))
                            d = score[:, blk(i + 1)]
                            nc.gpsimd.affine_select(out=d, in_=d, compare_op=ALU.is_ge, fill=OUT_OF_REACH, base=0,
                                                    pattern=[[-1, P]], channel_multiplier=1).then_inc(a["masked"], 1)

            @block.scalar
            def _(act):
                f = hT[0:HEADS, EV_MISC, :]
                cf = A["place"]["b_f"]
                nc.scalar.activation(lf[:, 0, :], f, ACT.Abs, bias=cols[0:HEADS, cf:cf + 1]).then_inc(a["lsig"], 1)
                act.wait_ge(a["lsig"], 1)
                nc.scalar.activation(lf[:, 1, :], lf[:, 0, :], ACT.Exp, scale=-1.0).then_inc(a["lsig"], 1)
                act.wait_ge(a["lsig"], 2)
                nc.scalar.activation(lf[:, 2, :], lf[:, 1, :], ACT.Ln, bias=1.0).then_inc(a["lsig"], 1)
                for h in range(HEADS):
                    act.wait_ge(a["spread"], h + 1)
                    nc.scalar.activation(ncum8[:, h, :], bank[h % 2][:, :], ACT.Copy, scale=-8.0).then_inc(a["spread_out"], 1)

                def b5_out(n, dst, scale=1.0):
                    act.wait_ge(a["b5"], n)
                    nc.scalar.activation(dst, bank[5][:, :].rearrange("p (h q) -> p h q", h=4), ACT.Copy,
                                         scale=scale).then_inc(a["b5_out"], 1)

                def queries_out(n, i, half):
                    b5_out(n, qlT[:, i % 2, 4 * half:4 * half + 4, :], float(HD) ** -0.5)

                def prob_out(i, k):
                    u = unit(i, k)
                    if k < HEADS:
                        dst = pTb[:, k % 2, 0:i + 1, :]
                        if i or k >= 2:
                            act.wait_ge(a["pv_b"], HEADS * i + k - 1)
                    else:
                        dst = pTa[:, 0:i + 1, k % 4, :]
                        if k == HEADS and i:
                            act.wait_ge(a["b5"], outputs(i - 1, ("a", 1)))
                        if k == HEADS + 4:
                            act.wait_ge(a["b5"], outputs(i, ("a", 0)))
                    act.wait_ge(a["prob_t"], u + 1)
                    src = bank[3 + u % 2][:, 0:(i + 1) * P].rearrange("s (j q) -> s j q", j=i + 1)
                    nc.scalar.activation(dst, src, ACT.Copy).then_inc(a["prob_out"], 1)

                for half in range(2):
                    queries_out(half + 1, 0, half)
                for s in range(UNITS * NB + 8):
                    i, k = s // UNITS, s % UNITS
                    if i < NB:
                        act.wait_ge(a["ttr"], s + 1)
                        t = tl[:, s % RING, 0:(i + 1) * P]
                        nc.scalar.activation(t, t, ACT.Exp, bias=stat[:, 0, s:s + 1], scale=-1.0,
                                             accum_out=stat[:, 1, s:s + 1]).then_inc(a["exp"], 1)
                        if k < HEADS and i + 1 < NB:
                            job, w = nth["s", i + 1, k], (i + 2) * P
                            act.wait_ge(a["logits"], job + 1)
                            n = HEADS * i + k
                            if n >= 2:
                                act.wait_ge(a["score"], n - 1)
                            nc.scalar.activation(rbuf[:, k % 2, 0:w], bank[job % 3][:, 0:w], ACT.Relu,
                                                 scale=float(D_IDX) ** -0.5).then_inc(a["relu"], 1)
                    if OUT <= s < UNITS * NB + OUT:
                        prob_out((s - OUT) // UNITS, (s - OUT) % UNITS)
                    if i + 1 < NB and k in (10, 12):
                        half = (k - 10) // 2
                        queries_out(outputs(i, ("q", half)), i + 1, half)
                    if i and k == 1:
                        b5_out(outputs(i - 1, ("a", 0)), oaT[:, 0:4, :])
                    if i and k == 5:
                        b5_out(outputs(i - 1, ("a", 1)), oaT[:, 4:8, :])
                    if i and k == 7:
                        b5_out(outputs(i - 1, ("o", 0)), xH[:, 0:4, blk(i - 1)])
                    if i < NB and k == HEADS + PV + 1:
                        act.wait_ge(a["pv_b"], HEADS * (i + 1))
                        nc.scalar.activation(xH[:, 4:8, blk(i)], bank[6][:, :].rearrange("p (h q) -> p h q", h=4),
                                             ACT.Copy).then_inc(a["o_b_hi"], 1)

            @block.vector
            def _(dve):
                for n in range(6):
                    dve.wait_ge(a["turned"], n + 1)
                    src = bank[3 + n % 2][:, :].rearrange("p (s c) -> p s c", s=NB)
                    if n == 0:
                        ins = nc.vector.tensor_copy(c_tm[:, :, :], src)
                    elif n < 5:
                        ins = nc.vector.tensor_copy(v_tm[:, :, (n - 1) * P:n * P], src)
                    else:
                        ins = nc.vector.tensor_scalar(wtm[:, :, :], src[:, :, W_IDX_ROW:W_IDX_ROW + HEADS],
                                                      float(HEADS) ** -0.5, None, ALU.mult)
                    ins.then_inc(a["turned_out"], 1)
                cf = A["place"]["b_f"]
                nc.vector.tensor_scalar(cumf[:, :], hT[0:HEADS, EV_MISC, :], cols[0:HEADS, cf:cf + 1], 0.0,
                                        ALU.add, ALU.min).then_inc(a["cumf"], 1)
                dve.wait_ge(a["cumf"], 1)
                dve.wait_ge(a["lsig"], 3)
                nc.vector.tensor_tensor(lf[:, 0, :], cumf[:, :], lf[:, 2, :], ALU.subtract).then_inc(a["cumf"], 1)
                dve.wait_ge(a["cumf"], 2)
                nc.vector.tensor_tensor_scan(cumf[:, :], lf[:, 0, :], lf[:, 0, :], 0.0, ALU.add, ALU.bypass)\
                    .then_inc(a["cumf"], 1)
                dve.wait_ge(a["col"], 1)
                nc.vector.tensor_scalar(fq8[:, :, :], bank[5][:, 0:NB * HEADS].rearrange("p (i h) -> p i h", i=NB),
                                        float(HD) ** 0.5, None, ALU.mult).then_inc(a["col_out"], 1)
                tk = Steps(a["topk"])
                dve.wait_ge(a["causal"], 1)
                nc.vector.tensor_copy(mneg[:, 0:P], causal[:, :]).then_inc(a["mneg"], 1)

                def add_score(i, h):
                    n, S = HEADS * (i - 1) + h, score[:, 0:(i + 1) * P]
                    r = rbuf[:, h % 2, 0:(i + 1) * P]
                    dve.wait_ge(a["relu"], n + 1)
                    if h == 0:
                        ins = nc.vector.tensor_scalar(S, r, wtm[:, i, 0:1], None, ALU.mult)
                    else:
                        dve.wait_ge(a["score"], n)
                        ins = nc.vector.scalar_tensor_tensor(S, r, wtm[:, i, h:h + 1], S, ALU.mult, ALU.add)
                    ins.then_inc(a["score"], 1)

                def select(i, rounds):
                    S = score[:, 0:(i + 1) * P]
                    for _ in range(rounds):
                        dve.wait_ge(a["topk"], tk.mark(nc.vector.max(top8[:, :], S)))
                        dve.wait_ge(a["topk"], tk.mark(nc.vector.match_replace(S, top8[:, :], S, MARK)))

                def o_low(src, i, half, done, number, sig):
                    dve.wait_ge(done, number)
                    nc.vector.tensor_tensor(xL[:, half, blk(i)], src[:, :].rearrange("p (h q) -> p h q", h=4),
                                            xH[:, half, blk(i)].bitcast(F32), ALU.subtract).then_inc(sig, 1)

                rounds = TOPK // 8
                mod_step = (mod_n - mod_first) // NB
                first_step = HEADS + 1
                for s in range(UNITS * NB + 9):
                    i, k = s // UNITS, s % UNITS
                    v = s - 2
                    if 0 <= v < UNITS * NB:
                        dve.wait_ge(a["exp"], v + 1)
                        nc.vector.reciprocal(stat[:, 2, v:v + 1], stat[:, 1, v:v + 1]).then_inc(a["recip"], 1)
                    if i < NB:
                        w = (i + 1) * P
                        kind, _, h = job_of(i, k)
                        job = nth[kind, i, h]
                        dve.wait_ge(a["logits"], job + 1)
                        dve.wait_ge(a["addend"], s + 1)
                        if s >= RING:
                            dve.wait_ge(a["prob_t"], s - RING + 1)
                        nc.vector.tensor_tensor_reduce(
                            out=tl[:, s % RING, 0:w], in0=bank[job % 3][:, 0:w], in1=Xa[:, s % 3, 0:w],
                            scale=-1.0 if kind == "a" else -float(HD) ** -0.5, scalar=3.0e38, op0=ALU.add, op1=ALU.min,
                            accum_out=stat[:, 0, s:s + 1]).then_inc(a["ttr"], 1)
                    if 0 <= v < UNITS * NB:
                        dve.wait_ge(a["recip"], v + 1)
                        t = tl[:, v % RING, 0:(v // UNITS + 1) * P]
                        nc.vector.tensor_scalar(t, t, stat[:, 2, v:v + 1], None, ALU.mult).then_inc(a["norm"], 1)
                    if i + 1 < NB:
                        if 1 <= k <= HEADS:
                            add_score(i + 1, k - 1)
                        if k == first_step:
                            dve.wait_ge(a["masked"], i + 1)
                        if k >= first_step:
                            steps = UNITS - first_step
                            select(i + 1, rounds * (k - first_step + 1) // steps - rounds * (k - first_step) // steps)
                        if k == UNITS - 1:
                            dve.wait_ge(a["addend"], UNITS * (i + 1))
                            S = score[:, 0:(i + 2) * P]
                            nc.vector.tensor_scalar(mneg[:, 0:(i + 2) * P], S, MARK, NEG, ALU.not_equal, ALU.mult)\
                                .then_inc(a["mneg"], 1)
                    if i < NB and k < mod_step:
                        c = mod_first + mod_step * i + k
                        dve.wait_ge(mod_rest[c % RAW], 16 * ((c - mod_first) // RAW + 1))
                        w = raw[:, c % RAW, 0:D]
                        row_sums(w, csil, modT[:, c, 0:1], w).then_inc(mod_used, 1)
                    if i < NB and k == HEADS + PV + 2:
                        o_low(bank[6], i, slice(4, 8), a["o_b_hi"], i + 1, a["o_b_lo"])
                    if i and k == 8:
                        o_low(bank[5], i - 1, slice(0, 4), a["b5_out"], outputs(i - 1, ("o", 0)), a["o_a_lo"])
                bm = A["place"]["b_mod"]
                dve.wait_ge(mod_used, mod_n)
                for v, n in enumerate((mod_n, mod_ctx)):
                    nc.vector.tensor_tensor(modT[:, 0:n, v], modT[:, 0:n, v], cols[:, bm:bm + n], ALU.add).then_inc(a["mod_evac"], 1)
                dve.wait_ge(a["mod_evac"], 2)
                for n, (scale, v, g) in enumerate(((8, 0, "g1"), (32, 0, "g2"), (8, 1, "g1"))):
                    g0 = A["place"][g]
                    nc.vector.scalar_tensor_tensor(gmod[:, n, :], modT[:, scale:scale + KD, v], 1.0, cols[:, g0:g0 + KD],
                                                   ALU.add, ALU.mult).then_inc(a["mod_evac"], 1)

            @block.tensor
            def _(pe):
                for n, t in enumerate((EV_CKV, EV_VB, EV_VB + 1, EV_VB + 2, EV_VB + 3, EV_MISC)):
                    if n >= 2:
                        pe.wait_ge(a["turned_out"], n - 1)
                    for s in range(NB):
                        mm = nc.tensor.transpose(bank[3 + n % 2][:, blk(s)], hT[:, t, blk(s)], ident[:, :])
                    mm.then_inc(a["turned"], 1)
                pe.wait_ge(a["cumf"], 3)
                for h in range(HEADS):
                    if h >= 2:
                        pe.wait_ge(a["spread_out"], h - 1)
                    nc.tensor.matmul(bank[h % 2][:, :], ident[0:HEADS, h:h + 1].to_broadcast([HEADS, P]), cumf[:, :],
                                     start=True, stop=True).then_inc(a["spread"], 1)
                for i in range(NB):
                    mm = nc.tensor.transpose(bank[5][:, i * HEADS:(i + 1) * HEADS], cumf[:, blk(i)], ident[0:HEADS, 0:HEADS])
                mm.then_inc(a["col"], 1)
                pe.wait_ge(a["par"], 32)

                def logits(kind, i, h):
                    n, w = nth[kind, i, h], (i + 1) * P
                    if n >= 3:
                        k0, i0, h0 = jobs[n - 3]
                        if k0 == "s":
                            pe.wait_ge(a["relu"], HEADS * (i0 - 1) + h0 + 1)
                        else:
                            pe.wait_ge(a["ttr"], unit(i0, h0 + (HEADS if k0 == "a" else 0)) + 1)
                    elif n < 3:
                        pe.wait_ge(a["spread_out"], HEADS)
                    if kind == "s":
                        l, r = hT[rows(h), EV_QI + h // 2, blk(i)], hT[rows(h), EV_KI, 0:w]
                    elif kind == "b":
                        l, r = hT[rows(h), EV_QB + h // 2, blk(i)], hT[rows(h), EV_KB + h // 2, 0:w]
                    else:
                        if h == 0:
                            pe.wait_ge(a["b5_out"], outputs(i - 1, ("q", 1)) if i else 2)
                        l, r = qlT[:, i % 2, 4 * (h % 2) + h // 2, :], hT[:, EV_CKV, 0:w]
                    nc.tensor.matmul(bank[n % 3][:, 0:w], l, r, start=True, stop=True).then_inc(a["logits"], 1)

                def turn(i, k):
                    u = unit(i, k)
                    pe.wait_ge(a["norm"], u + 1)
                    if u >= 2:
                        pe.wait_ge(a["prob_out"], u - 1)
                    else:
                        pe.wait_ge(a["turned_out"], 6)
                    for j in range(i + 1):
                        mm = nc.tensor.transpose(bank[3 + u % 2][:, blk(j)], tl[:, u % RING, blk(j)], ident[:, :])
                    mm.then_inc(a["prob_t"], 1)

                def values_b(i, h):
                    pe.wait_ge(a["prob_out"], unit(i, h) + 1)
                    if h == 0 and i:
                        pe.wait_ge(a["o_b_lo"], i)
                    for j in range(i + 1):
                        mm = nc.tensor.matmul(bank[6][rows(h), blk(h // 2)], v_tm[:, j, h * HD:(h + 1) * HD],
                                              pTb[:, h % 2, j, :], start=j == 0, stop=j == i)
                    mm.then_inc(a["pv_b"], 1)

                def values_a(i, g):
                    pe.wait_ge(a["b5_out"], outputs(i, ("a", g)) - 1)
                    if g == 0 and i == NB - 1:
                        pe.wait_ge(a["o_a_lo"], i)
                    pe.wait_ge(a["prob_out"], unit(i, HEADS + 4 * g + 3) + 1)
                    for j in range(i + 1):
                        mm = nc.tensor.matmul(bank[5][:, :], c_tm[:, j, :], pTa[:, j, :, :], start=j == 0, stop=j == i)
                    mm.then_inc(a["b5"], 1)

                def queries(i, half):
                    for h in range(half, HEADS, 2):
                        mm = nc.tensor.matmul(bank[5][:, blk(h // 2)], w_uk[rows(h), h // 2, :],
                                              hT[rows(h), EV_QA + h // 2, blk(i)], start=True, stop=True)
                    mm.then_inc(a["b5"], 1)

                def outputs_a(i):
                    pe.wait_ge(a["b5_out"], outputs(i, ("a", 1)))
                    for h in range(HEADS):
                        mm = nc.tensor.matmul(bank[5][rows(h), blk(h // 2)], w_uv[:, h, :], oaT[:, h, :],
                                              start=True, stop=True)
                    mm.then_inc(a["b5"], 1)

                pe.wait_ge(a["col_out"], 1)
                queries(0, 0)
                pe.wait_ge(a["b5_out"], 1)
                queries(0, 1)
                for s in range(UNITS * NB + 8):
                    i, k = s // UNITS, s % UNITS
                    if i and k == 0:
                        values_a(i - 1, 0)
                    if i < NB:
                        logits(*job_of(i, k))
                        if k < HEADS and i + 1 < NB:
                            logits("s", i + 1, k)
                    if TURN <= s < UNITS * NB + TURN:
                        turn((s - TURN) // UNITS, (s - TURN) % UNITS)
                    if s >= PV and (s - PV) // UNITS < NB and (s - PV) % UNITS < HEADS:
                        values_b((s - PV) // UNITS, (s - PV) % UNITS)
                    if i + 1 < NB and k in (9, 11):
                        half = (k - 9) // 2
                        pe.wait_ge(a["b5_out"], outputs(i, ("q", half)) - 1)
                        if half == 0 and i:
                            pe.wait_ge(a["o_a_lo"], i)
                        queries(i + 1, half)
                    if i and k == 4:
                        values_a(i - 1, 1)
                    if i and k == 6:
                        outputs_a(i - 1)

        HID = ARENA
        hidH, at = sb("hidH", [P, NFF, T], F32R, at=HID)
        hidL, at = sb("hidL", [P, NFF, T], F32R, at=at)
        scratch = at - 9 * T * 4
        sq, at_s = sb("sq", [P, 2, T], at=scratch)
        rstd, at_s = sb("rstd", [P, T], at=at_s)
        yt, at_s = sb("y", [P, 3, T], at=at_s)
        ht, at_s = sb("h", [P, 3, T], at=at_s)
        zsum, at = sb("zsum", [P, T], at=at)
        ab, at = sb("gate_value", [P, 2, T], at=at)
        hid, at = sb("hid", [P, T], at=at)


        s_zsum = sem("z_summed")
        s_out = [sem(f"stored{s}") for s in range(3)]
        nm = {n: sem("norm_" + n) for n in ("mean", "xc", "sq", "sum", "rstd", "y", "affine", "high")}
        count = dict.fromkeys([*nm, "zsum", "tap", "conv", "silu", "hid", "hid_hi", "hid_lo", "warm"], 0)
        ff = {n: sem("ffn_" + n) for n in ("tap", "conv", "silu", "hid", "hid_hi", "hid_lo")}

        def take(name, n):
            count[name] += n
            return count[name] - n

        class Residual(Stage):

            def __init__(self, w, right, per, gate=None, hidden=None):
                super().__init__(w, right, per)
                self.gate, self.hidden = gate, hidden
                self.z0 = take("zsum", 0 if gate is not None else KD + 1)

            def tensor(self, pe):
                if self.hidden is not None:
                    pe.wait_ge(ff["hid_lo"], self.hidden)
                super().tensor(pe)

            def scalar(self, act):
                self.first_high(act)
                chunks(act, self.w.n, lambda i, j, ahead: split_high(act, self.w, i, j + SPLIT) if ahead else None)

            def vector(self, dve):
                self.first_low(dve)
                if self.gate is None:
                    nc.vector.memset(zsum[:, :], 0.0).then_inc(s_zsum, 1)

                def tile(i, j, ahead):
                    b = self.bank_of(j)
                    if j % self.per == self.per - 1:
                        t0, nt = j // self.per, RAW // self.per
                        t = i * nt + t0
                        x = xT[:, t, :]
                        self.finished(dve, i, j)
                        if self.gate is None:
                            ins = nc.vector.scalar_tensor_tensor(x, x, ALPHA, bank[b][:, :], ALU.mult, ALU.add)
                        else:
                            ins = nc.vector.scalar_tensor_tensor(x, bank[b][:, :], modT[:, i * nt + (self.gate + t0), 0:1], x,
                                                                 ALU.mult, ALU.add)
                        self.emptied(ins, j)
                        if self.gate is None:
                            dve.wait_ge(acc_free[b], self.free_at(i, j) + 1)
                            dve.wait_ge(s_zsum, i * nt + (self.z0 + t0 + 1))
                            nc.vector.tensor_tensor(zsum[:, :], zsum[:, :], x, ALU.add).then_inc(s_zsum, 1)
                    if ahead:
                        split_low(dve, self.w, i, j + SPLIT)
                chunks(dve, self.w.n, tile)

        class Norm(Part):

            def __init__(self, kind, x, gain, shift, eps, right=None, ready=None, n=T, source=None, z0=0):
                self.kind, self.x, self.gain, self.shift, self.eps, self.n = kind, x, gain, shift, eps, n
                self.right, self.source = right, source
                self.c = {"mean": take("mean", kind == "ln"), "xc": take("xc", KD if kind == "ln" else 0),
                          "rstd": take("rstd", 2), "high": take("high", KD if right else 0)}
                self.c |= {m: take(m, KD) for m in ("sq", "sum", "y", "affine")}
                self.z0 = count["zsum"]
                self.ready = ready

            def at(self, name, t):
                return self.c[name] + t + 1

            def tensor(self, pe):
                if self.kind == "ln":
                    pe.wait_ge(s_zsum, self.z0)
                    nc.tensor.matmul(bank[6][:, 0:self.n], mean_of[:, :], zsum[:, 0:self.n], start=True, stop=True)\
                        .then_inc(nm["mean"], 1)
                if self.c["rstd"]:
                    pe.wait_ge(nm["rstd"], self.c["rstd"])
                for t in range(KD):
                    pe.wait_ge(nm["sq"], self.at("sq", t))
                    nc.tensor.matmul(bank[7][:, 0:self.n], mean_of[:, :], sq[:, t % 2, 0:self.n],
                                     start=t == 0, stop=t == KD - 1).then_inc(nm["sum"], 1)

            def scalar(self, act):
                for t in range(KD):
                    if self.kind == "ln":
                        act.wait_ge(nm["xc"], self.at("xc", t))
                    elif self.source:
                        act.wait_ge(*self.source(t))
                    if t >= 2:
                        act.wait_ge(nm["sum"], self.at("sum", t - 2))
                    nc.scalar.activation(sq[:, t % 2, 0:self.n], self.x[:, t, :], ACT.Square).then_inc(nm["sq"], 1)
                act.wait_ge(nm["sum"], self.at("sum", KD - 1))
                e = A["place"]["eps"] + self.eps
                nc.scalar.activation(rstd[:, 0:self.n], bank[7][:, 0:self.n], ACT.Ln, bias=cols[:, e:e + 1]).then_inc(nm["rstd"], 1)
                act.wait_ge(nm["rstd"], self.at("rstd", 0))
                nc.scalar.activation(rstd[:, 0:self.n], rstd[:, 0:self.n], ACT.Exp, scale=-0.5).then_inc(nm["rstd"], 1)
                if self.right:
                    for t in range(KD):
                        act.wait_ge(nm["y"], self.at("y", t))
                        nc.scalar.activation(self.right[0][:, t, :], yt[:, t % 3, 0:self.n], ACT.Identity, bias=self.shift(t),
                                             scale=self.gain(t)).then_inc(nm["high"], 1)

            def vector(self, dve):
                if self.kind == "ln":
                    dve.wait_ge(nm["mean"], self.at("mean", 0))
                    for t in range(KD):
                        nc.vector.tensor_tensor(self.x[:, t, :], self.x[:, t, :], bank[6][:, 0:self.n], ALU.subtract)\
                            .then_inc(nm["xc"], 1)
                dve.wait_ge(nm["rstd"], self.at("rstd", 1))
                for t in range(KD + 1):
                    if t < KD:
                        if t >= 3:
                            dve.wait_ge(nm["affine"], self.at("affine", t - 3))
                            if self.right:
                                dve.wait_ge(nm["high"], self.at("high", t - 3))
                        nc.vector.tensor_tensor(yt[:, t % 3, 0:self.n], self.x[:, t, :], rstd[:, 0:self.n], ALU.mult)\
                            .then_inc(nm["y"], 1)
                    if t and self.right:
                        v = t - 1
                        dve.wait_ge(nm["affine"], self.at("affine", v))
                        dve.wait_ge(nm["high"], self.at("high", v))
                        full = self.x[:, v, :] if self.kind == "ln" else ht[:, v % 3, 0:self.n]
                        nc.vector.tensor_tensor(self.right[1][:, v, :], full, self.right[0][:, v, :].bitcast(F32),
                                                ALU.subtract).then_inc(self.ready[0], 1)

            def gpsimd(self, pool):
                for t in range(KD):
                    pool.wait_ge(nm["y"], self.at("y", t))
                    dst = self.x[:, t, :] if self.kind == "ln" else ht[:, t % 3, 0:self.n]
                    if self.kind == "rms" and t >= 3:
                        pool.wait_ge(self.ready[0], self.ready[1] + t - 2)
                    if self.kind == "final":
                        if t >= 3:
                            pool.wait_ge(s_out[t % 3], 16 * (t // 3))
                        ins = nc.gpsimd.tensor_scalar(dst, yt[:, t % 3, :], self.gain(t), 1.0, ALU.mult, ALU.mult)
                    else:
                        ins = nc.gpsimd.tensor_scalar(dst, yt[:, t % 3, 0:self.n], self.gain(t), self.shift(t), ALU.mult, ALU.add)
                    ins.then_inc(nm["affine"], 1)

        class Up(Stage):

            def __init__(self, w, x_base, taps=None):
                super().__init__(w, X, 1, x_base)
                self.taps, self.n = taps, take("warm", 1)
                conv = taps is not None
                self.c = {n: take(n, m) for n, m in (("tap", 2 * NFF * conv), ("conv", 2 * NFF * conv), ("silu", NFF * conv),
                                                     ("hid", NFF * conv), ("hid_hi", NFF), ("hid_lo", NFF))}
                self.done = self.c["hid_lo"] + NFF

            def pair(self, name, i, j):
                return i * 2 + (self.c[name] + j // 2 + 1)

            def tap(self, i, j, n):
                return col[:, i * (3 * RAW) + (self.taps + 3 * j + n), :]

            def scalar(self, act):
                nc.scalar.activation(warm[:, self.n:self.n + 1], cols[:, 0:1], ACT.Silu)
                self.first_high(act)

                def tile(i, j, ahead):
                    gate, value = ab[:, 0, :], ab[:, 1, :]
                    if self.taps is None:
                        if j % 2 == 0:
                            self.finished(act, i, j)
                            self.emptied(nc.scalar.activation(gate, bank[0][:, :], ACT.Silu), j)
                    else:
                        if j % 2:
                            act.wait_ge(acc_free[0], self.free_at(i, j - 1) + 1)
                            nc.scalar.activation(gate, gate, ACT.Silu).then_inc(ff["silu"], 1)
                        self.finished(act, i, j)
                        nc.scalar.activation(value if j % 2 else gate, bank[j % 2][:, :], ACT.Copy,
                                             scale=self.tap(i, j, 2)).then_inc(ff["tap"], 1)
                    if ahead:
                        split_high(act, self.w, i, j + SPLIT)
                    if j % 2:
                        if self.taps is None:
                            act.wait_ge(acc_free[1], self.free_at(i, j) + 1)
                        else:
                            act.wait_ge(ff["hid"], self.pair("hid", i, j))
                        nc.scalar.activation(hidH[:, i * 2 + j // 2, :], hid[:, :], ACT.Copy).then_inc(ff["hid_hi"], 1)
                chunks(act, self.w.n, tile)

            def vector(self, dve):
                self.first_low(dve)

                def tile(i, j, ahead):
                    b = j % 2
                    if self.taps is not None:
                        acc, y = bank[b], ab[:, b, :]
                        dve.wait_ge(ff["tap"], i * RAW + (self.c["tap"] + j + 1))
                        nc.vector.scalar_tensor_tensor(y[:, 1:T], acc[:, 0:T - 1], self.tap(i, j, 1), y[:, 1:T],
                                                       ALU.mult, ALU.add).then_inc(ff["conv"], 1)
                        dve.wait_ge(ff["conv"], i * RAW + (self.c["conv"] + j + 1))
                        self.emptied(nc.vector.scalar_tensor_tensor(y[:, 2:T], acc[:, 0:T - 2], self.tap(i, j, 0), y[:, 2:T],
                                                                    ALU.mult, ALU.add), j)
                    if b:
                        if self.taps is None:
                            dve.wait_ge(acc_free[0], self.free_at(i, j - 1) + 1)
                            self.finished(dve, i, j)
                            dve.wait_ge(ff["hid_lo"], self.pair("hid_lo", i, j) - 1)
                            self.emptied(nc.vector.tensor_tensor(hid[:, :], ab[:, 0, :], bank[1][:, :], ALU.mult), j)
                        else:
                            dve.wait_ge(ff["silu"], self.pair("silu", i, j))
                            dve.wait_ge(acc_free[1], self.free_at(i, j) + 1)
                            nc.vector.tensor_tensor(hid[:, :], ab[:, 0, :], ab[:, 1, :], ALU.mult).then_inc(ff["hid"], 1)
                    if ahead:
                        split_low(dve, self.w, i, j + SPLIT)
                    if b:
                        t = i * 2 + j // 2
                        dve.wait_ge(ff["hid_hi"], self.pair("hid_hi", i, j))
                        nc.vector.tensor_tensor(hidL[:, t, :], hid[:, :], hidH[:, t, :].bitcast(F32), ALU.subtract)\
                            .then_inc(ff["hid_lo"], 1)
                chunks(dve, self.w.n, tile)

        class Store(Part):

            def __init__(self, norm):
                self.norm = norm

            def sync(self, sp):
                for t in range(KD):
                    sp.wait_ge(nm["affine"], self.norm.at("affine", t))
                    sp.dma_start(out[:, t, :], ht[:, t % 3, :]).then_inc(s_out[t % 3], 16)
                for s in range(3):
                    sp.wait_ge(s_out[s], 16 * len(range(s, KD, 3)))

        col = cols[:, :].unsqueeze(2)

        def param(name, n=1):
            return lambda t: col[:, A["place"][name] + t, :]

        def run(stages):
            with nc.Block() as block:
                @block.sync
                def _(sp):
                    for s in stages:
                        s.sync(sp)

                @block.scalar
                def _(act):
                    for s in stages:
                        s.scalar(act)

                @block.vector
                def _(dve):
                    for s in stages:
                        s.vector(dve)

                @block.tensor
                def _(pe):
                    for s in stages:
                        s.tensor(pe)

                @block.gpsimd
                def _(pool):
                    for s in stages:
                        s.gpsimd(pool)

        od_hT, _ = sb("od_hT", [P, OD_N, T], at=ARENA)

        def layer(l, out_name, proj):
            n = [Residual(W[out_name], X, 1)]
            n.append(Norm("ln", xT, param(f"ln_g{l}0"), param(f"ln_b{l}0"), 0, X, (x_ready, take("x_ready", KD))))
            n.append(Up(W[f"up{l}"], n[1].ready[1], A["place"][f"conv{l}"]))
            n.append(Residual(W[f"down{l}"], (hidH, hidL), 2, hidden=n[2].done))
            return n

        count["x_ready"] = KD
        stages = layer(0, "ev_out", None)
        stages.append(Norm("ln", xT, param("ln_g01"), param("ln_b01"), 0, X, (x_ready, take("x_ready", KD))))
        stages.append(Project(W["od_in"], od_hT, stages[-1].ready[1]))
        run(stages)

        at = ARENA + OD_N * T * 4
        sgu_w, at = sb("sgu_w", [P, HEADS, P], at=at)
        sgu_b, at = sb("sgu_b", [P, 4, P], at=at)
        sgu_g, at = sb("sgu_g", [P, HEADS * HD], at=at)
        vtm, at = sb("v_gated", [P, NB, HEADS * HD], at=at)
        vsq, at = sb("v_square", [P, NB, HEADS * HD], at=at)
        vst, at = sb("v_stat", [P, 3, NB * HEADS], at=at)
        mixb, at = sb("mixed", [P, 2, T], at=at)
        o = {n: sem("odd_" + n) for n in ("par", "tril", "gelu_v", "gelu_u", "turned", "out", "own", "square", "rstd", "gz", "tap",
                                          "mix", "full", "high")}

        self_normed = []
        cT, _ = sb("cT", [P, KD, LC], at=ARENA + 2 * NFF * T * 4)
        c_ready, s_ctx = sem("c_ready"), sem("ctx_in")
        cH, ctop = sb("cH", [P, KD, LC], F32R, at=ARENA + (2 * NFF + 4) * T * 4)
        cL, ctop = sb("cL", [P, KD, LC], F32R, at=ctop)
        assert at <= scratch
        ctx_norm = Norm("rms", cT, lambda t: gmod[:, 2, t:t + 1], lambda t: modT[:, t, 1:2], 1, (cH, cL), (c_ready, 0), n=LC,
                        source=lambda t: (s_ctx, 16))

        def groups(t):
            return t[:, :, :].rearrange("p c (g d) -> p (c g) d", g=HEADS)

        def per_group(n):
            return vst[:, n, :].unsqueeze(2).to_broadcast([P, NB * HEADS, HD])

        with nc.Block() as block:
            @block.sync
            def _(sp):
                sp.dma_start(cT[:, :, :], A["cT"]).then_inc(s_ctx, 16)
                sp.dma_start(sgu_w[:, :, :], A["sgu_w"]).then_inc(o["par"], 16)
                sp.dma_start(sgu_b[:, :, :], A["sgu_b"]).then_inc(o["par"], 16)
                sp.dma_start(sgu_g[:, :], A["sgu_g"]).then_inc(o["par"], 16)

            @block.gpsimd
            def _(pool):
                for m in range(4):
                    z = od_hT[:, OD_Z + m, :]
                    nc.gpsimd.tensor_tensor(z, z, od_hT[:, OD_GC + m, :], ALU.mult).then_inc(o["gz"], 1)
                pool.wait_ge(o["par"], 48)
                nc.gpsimd.affine_select(out=sgu_w[:, :, :], in_=sgu_w[:, :, :], compare_op=ALU.is_ge, fill=0.0, base=0,
                                        pattern=[[0, HEADS], [1, P]], channel_multiplier=-1).then_inc(o["tril"], 1)
                ctx_norm.gpsimd(pool)

            @block.scalar
            def _(act):
                for m in range(4):
                    v = od_hT[:, OD_V + m, :]
                    nc.scalar.activation(v, v, ACT.Gelu_apprx_tanh).then_inc(o["gelu_v"], 1)
                for m in range(4):
                    u = od_hT[:, OD_U + m, :]
                    nc.scalar.activation(u, u, ACT.Gelu_apprx_tanh).then_inc(o["gelu_u"], 1)
                k = A["place"]["od_conv"]
                for m in range(4):
                    act.wait_ge(o["gz"], m + 1)
                    nc.scalar.activation(od_hT[:, OD_GC + m, :], od_hT[:, OD_Z + m, :], ACT.Copy,
                                         scale=col[:, k + 3 * m + 2, :]).then_inc(o["tap"], 1)
                act.wait_ge(o["own"], 7)
                nc.scalar.activation(vsq[:, :, :], vtm[:, :, :], ACT.Square).then_inc(o["square"], 1)
                act.wait_ge(o["own"], 12)
                e = A["place"]["eps"]
                nc.scalar.activation(vst[:, 2, :], vst[:, 1, :], ACT.Ln, bias=cols[:, e:e + 1], scale=1.0 / HD).then_inc(o["rstd"], 1)
                act.wait_ge(o["rstd"], 1)
                nc.scalar.activation(vst[:, 2, :], vst[:, 2, :], ACT.Exp, scale=-0.5).then_inc(o["rstd"], 1)
                for n in range(8):
                    act.wait_ge(o["full"], n + 1)
                    src, t = (OD_GB + n, 4 + n) if n < 4 else (OD_U + n - 4, n - 4)
                    nc.scalar.activation(xH[:, t, :], od_hT[:, src, :], ACT.Copy).then_inc(o["high"], 1)
                ctx_norm.scalar(act)

            @block.vector
            def _(dve):
                own = Steps(o["own"])
                k = A["place"]["od_conv"]

                def step(ins):
                    return own.mark(ins)

                def wait(n):
                    dve.wait_ge(o["own"], n)

                def conv(m):
                    dve.wait_ge(o["tap"], m + 1)
                    y, x = od_hT[:, OD_GC + m, :], od_hT[:, OD_Z + m, :]
                    wait(step(nc.vector.scalar_tensor_tensor(y[:, 1:T], x[:, 0:T - 1], col[:, k + 3 * m + 1, :], y[:, 1:T],
                                                             ALU.mult, ALU.add)))
                    return step(nc.vector.scalar_tensor_tensor(y[:, 2:T], x[:, 0:T - 2], col[:, k + 3 * m, :], y[:, 2:T],
                                                               ALU.mult, ALU.add))

                def low(n):
                    src, t = (OD_GB + n, 4 + n) if n < 4 else (OD_U + n - 4, n - 4)
                    dve.wait_ge(o["high"], n + 1)
                    nc.vector.tensor_tensor(xL[:, t, :], od_hT[:, src, :], xH[:, t, :].bitcast(F32), ALU.subtract)

                for m in range(4):
                    dve.wait_ge(o["turned"], m + 1)
                    n = step(nc.vector.tensor_copy(vtm[:, :, m * P:(m + 1) * P],
                                                   bank[2 + m][:, :].rearrange("t (c d) -> t c d", c=NB)))
                wait(n)
                wait(step(nc.vector.tensor_reduce(vst[:, 0, :], groups(vtm), AX.X, ALU.add)))
                wait(step(nc.vector.tensor_scalar(vst[:, 0, :], vst[:, 0, :], 1.0 / HD, None, ALU.mult)))
                n_xc = step(nc.vector.tensor_tensor(groups(vtm), groups(vtm), per_group(0), ALU.subtract))
                assert n_xc == 7
                conv(0)
                conv(1)
                dve.wait_ge(o["square"], 1)
                n_var = step(nc.vector.tensor_reduce(vst[:, 1, :], groups(vsq), AX.X, ALU.add))
                assert n_var == 12
                conv(2)
                last_conv = conv(3)
                dve.wait_ge(o["rstd"], 2)
                wait(step(nc.vector.tensor_tensor(groups(vtm), groups(vtm), per_group(2), ALU.mult)))
                dve.wait_ge(o["par"], 48)
                normed = step(nc.vector.tensor_tensor(vtm[:, :, :], vtm[:, :, :],
                                                      sgu_g[:, :].unsqueeze(1).to_broadcast([P, NB, HEADS * HD]), ALU.mult))
                self_normed.append(normed)
                wait(last_conv)
                for m in range(4):
                    g = od_hT[:, OD_GB + m, :]
                    nc.vector.tensor_tensor(g, g, od_hT[:, OD_GC + m, :], ALU.mult).then_inc(o["full"], 1)
                for m in range(4):
                    low(m)
                for m in range(4):
                    dve.wait_ge(o["mix"], m + 1)
                    u, y = od_hT[:, OD_U + m, :], mixb[:, m % 2, :]
                    if m >= 2:
                        dve.wait_ge(o["full"], 4 + m - 1)
                    wait(step(nc.vector.tensor_tensor(y.rearrange("p (c t) -> p c t", c=NB),
                                                      bank[2 + m][:, :].rearrange("p (c t) -> p c t", c=NB),
                                                      sgu_b[:, m, :].unsqueeze(1).to_broadcast([P, NB, P]), ALU.add)))
                    dve.wait_ge(o["gelu_u"], m + 1)
                    nc.vector.tensor_tensor(u, u, y, ALU.mult).then_inc(o["full"], 1)
                    if m:
                        low(4 + m - 1)
                low(7)
                ctx_norm.vector(dve)

            @block.tensor
            def _(pe):
                for m in range(4):
                    pe.wait_ge(o["gelu_v"], m + 1)
                    for c in range(NB):
                        mm = nc.tensor.transpose(bank[2 + m][:, blk(c)], od_hT[:, OD_V + m, blk(c)], ident[:, :])
                    mm.then_inc(o["turned"], 1)
                pe.wait_ge(o["own"], self_normed[0])
                pe.wait_ge(o["tril"], 1)
                for g in range(HEADS):
                    for c in range(NB):
                        mm = nc.tensor.matmul(bank[2 + g // 2][rows(g), blk(c)], vtm[:, c, g * HD:(g + 1) * HD], sgu_w[:, g, :],
                                              start=True, stop=True)
                    if g % 2:
                        mm.then_inc(o["mix"], 1)
                ctx_norm.tensor(pe)

        stages = layer(1, "od_out", None)
        stages.append(Norm("ln", xT, param("ln_g11"), param("ln_b11"), 0))
        x_there = stages[-1]
        stages.append(Norm("rms", xT, lambda t: gmod[:, 0, t:t + 1], lambda t: modT[:, t, 0:1], 1, X,
                           (x_ready, take("x_ready", KD)), source=lambda t: (nm["affine"], x_there.at("affine", t))))
        sb_hT, at = sb("sb_hT", [P, SB_N, T], at=ARENA)
        sb_hc, at = sb("sb_hc", [P, SB_N - SB_CTX, LC], at=at)

        class ProjectBoth(Stage):

            def tensor(self, pe):
                w = self.w

                def tile(i, j, both):
                    pe.wait_ge(acc_free[j % 2], self.free_at(i, j))
                    pe.wait_ge(w.low, i * RAW + (w.c0 + j + 1))
                    mm = products(pe, w, j, self.right, bank[j % 2][:, :],
                                  x_ready=(x_ready, self.x_base) if not both and j == 0 else None)
                    if both:
                        mm = products(pe, w, j, (cH, cL), bank[2 + j % 2][:, 0:LC])
                    mm.then_inc(w.used, 1)
                tiles(pe, SB_CTX, lambda i, j: tile(i, j, False))
                tiles(pe, w.n, lambda i, j: tile(i, j, True), SB_CTX)

            def scalar(self, act):
                self.first_high(act)

                def tile(i, j, ahead, both):
                    self.finished(act, i, j)
                    if both:
                        nc.scalar.activation(sb_hc[:, i * RAW + (j - SB_CTX), :], bank[2 + j % 2][:, 0:LC], ACT.Copy)
                    self.emptied(nc.scalar.activation(sb_hT[:, i * RAW + j, :], bank[j % 2][:, :], ACT.Copy), j)
                    if ahead:
                        split_high(act, self.w, i, j + SPLIT)
                with act.Fori(0, SB_CTX // RAW) as i:
                    for j in range(RAW):
                        tile(i, j, True, False)
                chunks(act, self.w.n, lambda i, j, ahead: tile(i, j, ahead, True), SB_CTX)

            def vector(self, dve):
                self.first_low(dve)
                chunks(dve, self.w.n, lambda i, j, ahead: split_low(dve, self.w, i, j + SPLIT) if ahead else None)

        stages.append(ProjectBoth(W["sb_in"], X, 1, stages[-1].ready[1]))
        stages[-1].chain = False
        run(stages)

        NK = LC + T
        KT = NK // P
        at = ARENA + (SB_N * T + (SB_N - SB_CTX) * LC) * 4
        U7 = 2 * HG
        SLOT = CHUNK * 4
        kx, _ = sb("gla_k", [P, U7, T], at=raw_at)
        kc, at = sb("gla_kc", [P, U7, LC], at=at)
        lbs, at = sb("gla_lb", [P, 6, U7], at=at)
        gain_hg, at = sb("gla_gain", [P, 1], at=at)
        LEVELS = P.bit_length() - 1
        level_mask, at = sb("gla_masks", [P, 2, LEVELS * P], U8, at=at)
        KEPT = at
        rope, at = sb("rope", [P, 4, T], at=at)
        turn64, at = sb("rope_turn", [P, P], at=at)
        mean64, at = sb("mean_of_head", [P, P], at=at)
        kall, at = sb("keys", [P, NK], at=at)
        vall, at = sb("values", [P, KT, P], at=at)
        nrot, at = sb("head_rot", [P, 2, T], at=at)
        nsin, at = sb("head_sin", [P, 2, T], at=at)
        st2, at = sb("stat2", [P, 3, 32], at=at)
        nrs, _ = sb("head_rstd", [P, 6, T], at=at)
        pT2, at = sb("probs_t", [P, KT, 4, P], at=at)
        pr2, at2 = sb("probs2", [P, 4, NK], at=split_at)
        nsq, at2 = sb("head_sq", [P, 2, T], at=at2)
        inside, at2 = sb("gla_inside", [P, T], at=at2)
        masks_in = (sb("masks_in0", [P, LEVELS * P], at=raw_at + U7 * T * 4)[0], sb("masks_in1", [P, LEVELS * P], at=at2)[0])
        assert at2 + LEVELS * P * 4 <= split_end
        b = {n: sem("sec_" + n) for n in ("par", "sq", "mean", "rstd", "gain", "rot", "cos", "sin", "roped", "v_turned", "v_out",
                                          "logits", "max", "exp", "recip", "norm", "prob_t", "prob_out", "pv", "o_hi", "o_lo")}
        HIGH = PV + 1
        NT = 6

        g = {n: sem("gla_" + n) for n in (
            "par", "masks", "lb", "lb_exp", "inside", "sig", "silu", "fg", "k", "ln", "scan", "v_turned", "v_out", "diff", "exp",
            "mult", "level", "pred", "since", "to_end", "qe", "kd", "kd_turned", "kd_out", "kv", "state", "ksum", "diag",
            "diag_out", "o", "sq", "mean", "rstd", "y", "o_hi", "o_lo")}
        CTX_FF = SB_FF - SB_CTX

        def gate(u):
            return (u % 2) * HG + u // 2

        def bx(u):
            return sb_hT[:, SB_FF + gate(u), :]

        def bc(u):
            return sb_hc[:, CTX_FF + gate(u), :]

        def both(tile, d):
            return tile[:, d * HG:(d + 1) * HG, :]
        gates_x, gates_c = sb_hT[:, SB_FF:SB_FF + U7, :], sb_hc[:, CTX_FF:CTX_FF + U7, :]

        def lower_bounds(dve):
            lb = Steps(g["lb"])

            def step(ins):
                dve.wait_ge(g["lb"], lb.mark(ins))
            r = A["place"]["lb_raw"]
            raw0, raw1 = cols[:, r:r + U7], cols[:, r + U7:r + 2 * U7]
            step(nc.vector.tensor_tensor(lbs[:, 0, :], raw0, raw1, ALU.max))
            step(nc.vector.tensor_tensor(lbs[:, 1, :], raw0, lbs[:, 0, :], ALU.subtract))
            step(nc.vector.tensor_tensor(lbs[:, 2, :], raw1, lbs[:, 0, :], ALU.subtract))
            dve.wait_ge(g["lb_exp"], 1)
            step(nc.vector.tensor_tensor(lbs[:, 3, :], lbs[:, 1, :], lbs[:, 2, :], ALU.add))
            step(nc.vector.reciprocal(lbs[:, 4, :], lbs[:, 3, :]))
            step(nc.vector.tensor_tensor(lbs[:, 0, :], lbs[:, 1, :], lbs[:, 4, :], ALU.mult))
            step(nc.vector.tensor_scalar(lbs[:, 5, :], lbs[:, 0, :], -1.0, 1.0, ALU.mult, ALU.add))
            step(nc.vector.tensor_scalar(lbs[:, 0, :], lbs[:, 0, :], GATE_FLOOR, None, ALU.max))
            e = A["place"]["g_hg"]
            step(nc.vector.tensor_scalar(gain_hg[:, :], cols[:, e:e + 1], float(P) ** -0.5, None, ALU.mult))

        def sum_gates(dve, u):
            dve.wait_ge(g["ln"], 4)
            x, c = (bx(u), bc(u)) if u % 2 == 0 else (bx(u)[:, ::-1], bc(u)[:, ::-1])
            nc.vector.tensor_tensor_scan(x, inside[:, :], x, 0.0, ALU.mult, ALU.add).then_inc(g["scan"], 1)
            nc.vector.tensor_tensor_scan(c, c, c, 0.0, ALU.add, ALU.bypass).then_inc(g["scan"], 1)

        def head_tile(n):
            return sb_hT[:, SB_Q + n, :] if n < 4 else sb_hT[:, SB_K, :] if n == 4 else sb_hc[:, SB_K - SB_CTX, :]

        def width(n):
            return LC if n == 5 else T

        def mean_bank(n):
            return bank[n if n < 4 else n + 2][:, 0:width(n)]

        wide = psum[:, :]

        def logit_cols(u):
            return slice((u % 2) * 1024 + 256, (u % 2) * 1024 + 1024)

        def turns(u):
            return 3 * (u // 2) + (1 if u % 2 == 0 else 3)

        def out_low(dve, i):
            dve.wait_ge(b["o_hi"], i + 1)
            nc.vector.tensor_tensor(xL[:, 0:4, blk(i)], bank[7][:, :].rearrange("p (r q) -> p r q", r=4),
                                    xH[:, 0:4, blk(i)].bitcast(F32), ALU.subtract).then_inc(b["o_lo"], 1)

        U2 = 8 * NB
        with nc.Block() as block:
            @block.sync
            def _(sp):
                sp.dma_start(mean64[:, :], A["mean64"]).then_inc(b["par"], 16)
                sp.dma_start(turn64[:, :], A["turn64"]).then_inc(b["par"], 16)
                sp.dma_start(rope[:, :, :], A["rope"]).then_inc(b["par"], 16)
                for d in range(2):
                    sp.dma_start(masks_in[d][:, :], A["level_masks"][d]).then_inc(g["par"], 16)

            @block.gpsimd
            def _(pool):
                nc.gpsimd.memset(inside[:, :], 1.0).then_inc(g["inside"], 1)
                pool.wait_ge(g["inside"], 1)
                nc.gpsimd.memset(inside[:, :].rearrange("p (c t) -> p c t", c=NB)[:, :, 0:1], 0.0).then_inc(g["inside"], 1)
                for d in range(2):
                    for hd in range(HG):
                        u = 2 * hd + d
                        pool.wait_ge(g["fg"], 2 * gate(u) + 2)
                        nc.gpsimd.tensor_scalar(kx[:, u, :], bx(u), -1.0, 1.0, ALU.mult, ALU.add).then_inc(g["k"], 1)
                        nc.gpsimd.tensor_scalar(kc[:, u, :], bc(u), -1.0, 1.0, ALU.mult, ALU.add).then_inc(g["k"], 1)
                pool.wait_ge(b["par"], 48)
                for n in range(NT - 1):
                    pool.wait_ge(b["gain"], n + 1)
                    if n >= 2:
                        pool.wait_ge(b["roped"], n - 1)
                    nc.gpsimd.tensor_tensor(nrot[:, n % 2, :], head_tile(n), rope[:, 0 if n < 4 else 2, :], ALU.mult)\
                        .then_inc(b["cos"], 1)

            @block.scalar
            def _(act):
                e = A["place"]["eps"] + 1
                act.wait_ge(g["lb"], 3)
                nc.scalar.activation(lbs[:, 1:3, :], lbs[:, 1:3, :], ACT.Exp).then_inc(g["lb_exp"], 1)
                for d in range(2):
                    for t in (both(gates_x, d), both(gates_c, d)):
                        nc.scalar.activation(t, t, ACT.Sigmoid).then_inc(g["sig"], 1)
                for n in range(NT):
                    if n >= 2:
                        act.wait_ge(b["mean"], n - 1)
                    nc.scalar.activation(nsq[:, n % 2, 0:width(n)], head_tile(n), ACT.Square).then_inc(b["sq"], 1)
                for n in range(NT):
                    act.wait_ge(b["mean"], n + 1)
                    nc.scalar.activation(nrs[:, n, 0:width(n)], mean_bank(n), ACT.Ln, bias=cols[:, e:e + 1]).then_inc(b["rstd"], 1)
                for n in range(NT):
                    act.wait_ge(b["rstd"], n + 1)
                    r = nrs[:, n, 0:width(n)]
                    nc.scalar.activation(r, r, ACT.Exp, scale=-0.5).then_inc(b["rstd"], 1)
                for d in range(2):
                    act.wait_ge(g["k"], 2 * HG * (d + 1))
                    for t in (both(gates_x, d), both(gates_c, d)):
                        nc.scalar.activation(t, t, ACT.Ln).then_inc(g["ln"], 1)

                def prob_out(u):
                    r = u % 4
                    if u % 2 == 0 and u >= 4:
                        act.wait_ge(b["pv"], u // 2 - 1)
                    if u % 2:
                        act.wait_ge(b["prob_t"], turns(u) - 1)
                        src = bank[5][:, :].rearrange("s (r j q) -> s j r q", r=2, j=2)
                        nc.scalar.activation(pT2[:, 4:KT, r - 1:r + 1, :], src, ACT.Copy).then_inc(b["prob_out"], 1)
                    act.wait_ge(b["prob_t"], turns(u))
                    nc.scalar.activation(pT2[:, 0:4, r, :], bank[4 + u % 2 * 2][:, :].rearrange("s (j q) -> s j q", j=4),
                                         ACT.Copy).then_inc(b["prob_out"], 1)

                for u in range(U2 + HIGH + 1):
                    if OUT <= u < U2 + OUT:
                        prob_out(u - OUT)
                    if u < U2:
                        act.wait_ge(b["max"], u + 1)
                        if u >= 4:
                            act.wait_ge(b["prob_t"], turns(u - 4))
                        nc.scalar.activation(pr2[:, u % 4, :], wide[:, logit_cols(u)], ACT.Exp, bias=st2[:, 0, u:u + 1],
                                             accum_out=st2[:, 1, u:u + 1]).then_inc(b["exp"], 1)
                    if u == U2 + OUT:
                        x = sb_hT[:, SB_HQ:SB_HG + HG, :]
                        nc.scalar.activation(x, x, ACT.Silu).then_inc(g["silu"], 1)
                    if u >= HIGH and (u - HIGH) % 8 == 7:
                        i = (u - HIGH) // 8
                        act.wait_ge(b["pv"], 4 * i + 4)
                        nc.scalar.activation(xH[:, 0:4, blk(i)], bank[7][:, :].rearrange("p (r q) -> p r q", r=4), ACT.Copy)\
                            .then_inc(b["o_hi"], 1)

            @block.vector
            def _(dve):
                lower_bounds(dve)
                for t in range(U7):
                    dve.wait_ge(g["sig"], 2 * (t // HG) + 2)
                    for f in (sb_hT[:, SB_FF + t, :], sb_hc[:, CTX_FF + t, :]):
                        nc.vector.tensor_scalar(f, f, lbs[:, 5, t:t + 1], lbs[:, 0, t:t + 1], ALU.mult, ALU.add).then_inc(g["fg"], 1)
                for n in range(NT):
                    w = width(n)
                    dve.wait_ge(b["rstd"], NT + n + 1)
                    at_g = A["place"]["g_q" if n < 4 else "g_k"]
                    dst = kall[:, 0:LC] if n == 5 else head_tile(n)
                    nc.vector.scalar_tensor_tensor(dst, head_tile(n), cols[:, at_g:at_g + 1], nrs[:, n, 0:w], ALU.mult, ALU.mult)\
                        .then_inc(b["gain"], 1)
                    if 1 <= n:
                        v = n - 1
                        dve.wait_ge(b["rot"], v + 1)
                        if v >= 2:
                            dve.wait_ge(b["roped"], v - 1)
                        dve.wait_ge(b["par"], 48)
                        nc.vector.tensor_tensor(nsin[:, v % 2, :], bank[2 + v % 2][:, :], rope[:, 1 if v < 4 else 3, :], ALU.mult)\
                            .then_inc(b["sin"], 1)
                        dve.wait_ge(b["sin"], v + 1)
                        dve.wait_ge(b["cos"], v + 1)
                        dst = kall[:, LC:NK] if v == 4 else head_tile(v)
                        nc.vector.tensor_tensor(dst, nrot[:, v % 2, :], nsin[:, v % 2, :], ALU.add).then_inc(b["roped"], 1)
                for n in range(2):
                    dve.wait_ge(b["v_turned"], n + 1)
                    c = 2 if n == 0 else 4
                    nc.vector.tensor_copy(vall[:, 0:2, :] if n == 0 else vall[:, 2:6, :],
                                          bank[4 + n][:, 0:c * P].rearrange("s (j d) -> s j d", j=c)).then_inc(b["v_out"], 1)
                for u in range(U2 + HIGH + 2):
                    v = u - 2
                    if 0 <= v < U2:
                        dve.wait_ge(b["exp"], v + 1)
                        nc.vector.reciprocal(st2[:, 2, v:v + 1], st2[:, 1, v:v + 1]).then_inc(b["recip"], 1)
                    if u < U2:
                        dve.wait_ge(b["logits"], u + 1)
                        nc.vector.tensor_reduce(st2[:, 0, u:u + 1], wide[:, logit_cols(u)], AX.X, ALU.max, negate=True)\
                            .then_inc(b["max"], 1)
                    if 0 <= v < U2:
                        dve.wait_ge(b["recip"], v + 1)
                        t = pr2[:, v % 4, :]
                        nc.vector.tensor_scalar(t, t, st2[:, 2, v:v + 1], None, ALU.mult).then_inc(b["norm"], 1)
                    if u == 0:
                        dve.wait_ge(g["inside"], 2)
                    if u < U7:
                        sum_gates(dve, u)
                    elif u < U7 + 2:
                        dve.wait_ge(g["par"], 32)
                        nc.vector.tensor_copy(level_mask[:, u - U7, :], masks_in[u - U7][:, :]).then_inc(g["masks"], 1)
                    if u >= HIGH + 1 and (u - HIGH - 1) % 8 == 7:
                        out_low(dve, (u - HIGH - 1) // 8)

            @block.tensor
            def _(pe):
                pe.wait_ge(b["par"], 48)
                for s in range(2):
                    mm = nc.tensor.transpose(bank[4][:, blk(s)], sb_hc[:, SB_V - SB_CTX, blk(s)], ident[:, :])
                mm.then_inc(b["v_turned"], 1)
                for s in range(4):
                    mm = nc.tensor.transpose(bank[5][:, blk(s)], sb_hT[:, SB_V, blk(s)], ident[:, :])
                mm.then_inc(b["v_turned"], 1)
                for n in range(NT):
                    pe.wait_ge(b["sq"], n + 1)
                    nc.tensor.matmul(mean_bank(n), mean64[:, :], nsq[:, n % 2, 0:width(n)], start=True, stop=True)\
                        .then_inc(b["mean"], 1)
                for v in range(NT - 1):
                    pe.wait_ge(b["gain"], v + 1)
                    if v >= 2:
                        pe.wait_ge(b["sin"], v - 1)
                    else:
                        pe.wait_ge(b["rstd"], 4)
                    nc.tensor.matmul(bank[2 + v % 2][:, :], turn64[:, :], head_tile(v), start=True, stop=True)\
                        .then_inc(b["rot"], 1)
                pe.wait_ge(b["gain"], NT)
                pe.wait_ge(b["roped"], NT - 1)
                pe.wait_ge(b["v_out"], 2)

                def logits(u):
                    i, kv, r = u // 8, (u // 4) % 2, u % 4
                    if u >= 2:
                        pe.wait_ge(b["exp"], u - 1)
                    q = sb_hT[rows(kv), SB_Q + r, blk(i)]
                    c0 = (u % 2) * 1024
                    nc.tensor.matmul(wide[:, c0 + 256:c0 + 512], q, kall[rows(kv), 0:LC], start=True, stop=True)
                    nc.tensor.matmul(wide[:, c0 + 512:c0 + 1024], q, kall[rows(kv), LC:NK], start=True, stop=True)\
                        .then_inc(b["logits"], 1)

                def turn(u):
                    pe.wait_ge(b["norm"], u + 1)
                    if u >= 2:
                        pe.wait_ge(b["prob_out"], turns(u - u % 2 - 1))
                    for j in range(4, KT):
                        mm = nc.tensor.transpose(bank[5][:, blk(2 * (u % 2) + j - 4)], pr2[:, u % 4, blk(j)], ident[:, :])
                    if u % 2:
                        mm.then_inc(b["prob_t"], 1)
                    for j in range(4):
                        mm = nc.tensor.transpose(bank[4 + u % 2 * 2][:, blk(j)], pr2[:, u % 4, blk(j)], ident[:, :])
                    mm.then_inc(b["prob_t"], 1)

                def values(n):
                    kv, half = (n // 2) % 2, n % 2
                    pe.wait_ge(b["prob_out"], turns(2 * n + 1))
                    if n % 4 == 0 and n:
                        pe.wait_ge(b["o_lo"], n // 4)
                    for j in range(KT):
                        mm = nc.tensor.matmul(bank[7][rows(kv), half * 2 * P:(half + 1) * 2 * P], vall[:, j, kv * HD:(kv + 1) * HD],
                                              pT2[:, j, 2 * half:2 * half + 2, :], start=j == 0, stop=j == KT - 1)
                    mm.then_inc(b["pv"], 1)

                for u in range(U2 + HIGH):
                    if u < U2:
                        logits(u)
                    if TURN <= u < U2 + TURN:
                        turn(u - TURN)
                    if u >= PV and (u - PV) % 2:
                        values((u - PV) // 2)

        LAG = 3
        qe, at = sb("gla_q_decayed", [P, 4, T], at=KEPT)
        state, at = sb("gla_state", [P, 4, NB, P], at=at)
        kd_tm, at = sb("gla_kd_tm", [P, 5, P], at=at)
        mixed, at = sb("gla_mixed", [P, 4, T], at=at)
        aT, at = sb("gla_weights", [P, 2, NB, P], at=at)
        v_tm7, at2 = sb("gla_v_tm", [P, HG, NB + 2, P], at=split_at)
        dec, at2 = sb("gla_decay", [P, 4, T], at=at2)
        assert at2 <= split_end
        eb = sb_hT[:, SB_Q:SB_Q + 2, :]
        kds = (sb_hT[:, SB_Q + 2:SB_Q + 4, :].rearrange("p a t -> p (a t)")[:, 0:5 * P],
               sb_hT[:, SB_K:SB_K + 2, :].rearrange("p a t -> p (a t)")[:, 0:5 * P])
        ksum = sb_hT[:, SB_I, :]
        osq, ors, oy = (sb_hc[:, n:n + 2, :].rearrange("p a t -> p (a t)") for n in (0, 2, 4))
        def head_dir(u):
            return u // 2, u % 2

        def chunk_at(u, n):
            return n if u % 2 == 0 else NB - 1 - n

        def last(u, c, size=P):
            t = c * size + (size - 1 if u % 2 == 0 else 0)
            return slice(t, t + 1)

        def halves(ap, u, n):
            h = P >> (n + 1)
            v = ap.rearrange("p (b t) -> p b t", t=2 * h)
            low, high = v[:, :, 0:h], v[:, :, h:2 * h]
            if u % 2 == 0:
                return high, low, v[:, :, h - 1:h].to_broadcast([P, T // (2 * h), h])
            return low, high, v[:, :, h:h + 1].to_broadcast([P, T // (2 * h), h])

        JOBS = U7 * LEVELS
        scalar_reads = {(2 * hd + 2 + d, l): (hd, part) for hd in range(HG - 1) for part, d, l in ((0, 0, 6), (1, 1, 2), (2, 1, 5))}
        vector_reads = {(2 * hd + 3, l): (hd, part) for hd in range(HG - 1) for part, l in ((0, 4), (1, 6))}

        with nc.Block() as block:
            @block.sync
            def _(sp):
                w = W["sb_out"]
                for s in (RAW - 1, *range(RAW - 1)):
                    units = min(U7, -(-(s + 1) * SLOT // (T * 4)))
                    if s * SLOT < U7 * T * 4:
                        sp.wait_ge(g["mult"], units * LEVELS)
                    load_chunk(sp, w, s, s)

            @block.gpsimd
            def _(pool):
                def prepare(u):
                    hd, d = head_dir(u)
                    pool.wait_ge(g["to_end"], u + 1)
                    k = kds[u % 2]
                    x0 = d * P
                    nc.gpsimd.tensor_tensor(k[:, 0:3 * P], k[:, 0:3 * P], kx[:, u, x0:x0 + 3 * P], ALU.mult)
                    nc.gpsimd.tensor_tensor(k[:, 3 * P:5 * P], k[:, 3 * P:5 * P], kc[:, u, :], ALU.mult).then_inc(g["kd"], 1)
                def sum_keys(hd):
                    if hd:
                        pool.wait_ge(g["diag"], hd)
                    else:
                        pool.wait_ge(g["v_out"], 2 * HG)
                    nc.gpsimd.tensor_tensor(ksum, kx[:, 2 * hd, :], kx[:, 2 * hd + 1, :], ALU.add).then_inc(g["ksum"], 1)

                prepare(0)
                sum_keys(0)
                for n in range(JOBS):
                    u, l = n // LEVELS, n % LEVELS
                    hd, d = head_dir(u)
                    pool.wait_ge(g["exp"], n + 1)
                    if n >= 4:
                        pool.wait_ge(g["level"], n - 3)
                    eq, ek, _ = halves(dec[:, n % 4, :], u, l)
                    mq, mk, _ = halves(mixed[:, n % 4, :], u, l)
                    nc.gpsimd.tensor_tensor(mq, halves(sb_hT[:, SB_HQ + hd, :], u, l)[0], eq, ALU.mult)
                    nc.gpsimd.tensor_tensor(mk, halves(kx[:, u, :], u, l)[1], ek, ALU.mult).then_inc(g["mult"], 1)
                    if l == 2 and u + 1 < U7:
                        prepare(u + 1)
                    if l == 4 and d == 1 and hd + 1 < HG:
                        sum_keys(hd + 1)

            @block.scalar
            def _(act):
                def prepare(u):
                    d = u % 2
                    if u >= 2:
                        act.wait_ge(g["kd_turned"], u - 1)
                    k = kds[u % 2]
                    for p in range(3):
                        c = p + d
                        nc.scalar.activation(k[:, blk(p)], bx(u)[:, blk(c)], ACT.Exp, bias=bx(u)[:, last(u, c)], scale=-1.0)
                    nc.scalar.activation(k[:, 3 * P:5 * P], bc(u), ACT.Exp, bias=bc(u)[:, last(u, 0, LC)], scale=-1.0)\
                        .then_inc(g["to_end"], 1)
                    if u >= 2:
                        act.wait_ge(g["qe"], u - 1)
                        act.wait_ge(g["state"], 4 * (u - 1))
                    nc.scalar.activation(eb[:, u % 2, :], bx(u), ACT.Exp).then_inc(g["since"], 1)

                def kd_out(u):
                    act.wait_ge(g["kd_turned"], u + 1)
                    if u:
                        act.wait_ge(g["kv"], u)
                    nc.scalar.activation(kd_tm[:, 0:3, :], bank[3][:, 0:3 * P].rearrange("t (c k) -> t c k", c=3), ACT.Copy)
                    nc.scalar.activation(kd_tm[:, 3:5, :], bank[4][:, 0:2 * P].rearrange("t (c k) -> t c k", c=2), ACT.Copy)\
                        .then_inc(g["kd_out"], 1)

                def read_out(hd, part):
                    if part == 0:
                        act.wait_ge(g["o"], hd + 1)
                        nc.scalar.activation(osq, bank[6][:, :], ACT.Square, scale=HG_SCALE).then_inc(g["sq"], 1)
                    elif part == 1:
                        act.wait_ge(g["mean"], hd + 1)
                        if hd:
                            act.wait_ge(g["y"], 2 * hd)
                        e = A["place"]["eps"] + 1
                        nc.scalar.activation(ors, bank[7][:, :], ACT.Ln, bias=cols[:, e:e + 1]).then_inc(g["rstd"], 1)
                        act.wait_ge(g["rstd"], 2 * hd + 1)
                        nc.scalar.activation(ors, ors, ACT.Exp, scale=-0.5).then_inc(g["rstd"], 1)
                    else:
                        act.wait_ge(g["y"], 2 * hd + 2)
                        nc.scalar.activation(xH[:, 4 + hd, :], oy, ACT.Copy).then_inc(g["o_hi"], 1)

                prepare(0)
                for hd in range(HG):
                    act.wait_ge(g["v_turned"], 2 * hd + 2)
                    nc.scalar.activation(v_tm7[:, hd, 0:NB, :], bank[3][:, :].rearrange("t (c v) -> t c v", c=NB), ACT.Copy)\
                        .then_inc(g["v_out"], 1)
                    nc.scalar.activation(v_tm7[:, hd, NB:NB + 2, :], bank[4][:, 0:LC].rearrange("t (c v) -> t c v", c=2), ACT.Copy)\
                        .then_inc(g["v_out"], 1)
                for n in range(JOBS):
                    u, l = n // LEVELS, n % LEVELS
                    hd, d = head_dir(u)
                    act.wait_ge(g["diff"], n + 1)
                    e = dec[:, n % 4, :]
                    nc.scalar.activation(e, e, ACT.Exp).then_inc(g["exp"], 1)
                    if l == 1:
                        kd_out(u)
                    if l == 1 and d == 0:
                        act.wait_ge(g["diag"], hd + 1)
                        if hd >= 2:
                            act.wait_ge(g["o"], hd - 1)
                        nc.scalar.activation(aT[:, hd % 2, :, :], bank[7][:, :].rearrange("s (c t) -> s c t", c=NB), ACT.Copy)\
                            .then_inc(g["diag_out"], 1)
                    if l == 0 and u + 1 < U7:
                        prepare(u + 1)
                    if (u, l) in scalar_reads:
                        read_out(*scalar_reads[u, l])
                for part in range(3):
                    read_out(HG - 1, part)

            @block.vector
            def _(dve):
                def states(u):
                    dve.wait_ge(g["kv"], u + 1)
                    dve.wait_ge(g["since"], u + 1)
                    if u >= 4:
                        dve.wait_ge(g["o"], u // 2 - 1)
                    nc.vector.tensor_tensor(qe[:, u % 4, :], sb_hT[:, SB_HQ + u // 2, :], eb[:, u % 2, :], ALU.mult).then_inc(g["qe"], 1)
                    S = state[:, u % 4, :, :]
                    nc.vector.tensor_copy(S[:, 0, :], bank[5][:, 0:P]).then_inc(g["state"], 1)
                    for p in range(3):
                        dve.wait_ge(g["state"], 4 * u + p + 1)
                        nc.vector.scalar_tensor_tensor(S[:, p + 1, :], S[:, p, :], eb[:, u % 2, last(u, chunk_at(u, p))],
                                                       bank[5][:, blk(p + 1)], ALU.mult, ALU.add).then_inc(g["state"], 1)

                def read_out(hd, part):
                    if part == 0:
                        dve.wait_ge(g["rstd"], 2 * hd + 2)
                        if hd:
                            dve.wait_ge(g["o_lo"], hd)
                        nc.vector.scalar_tensor_tensor(oy, bank[6][:, :], gain_hg[:, :], ors, ALU.mult, ALU.mult).then_inc(g["y"], 1)
                        dve.wait_ge(g["y"], 2 * hd + 1)
                        nc.vector.tensor_tensor(oy, oy, sb_hT[:, SB_HG + hd, :], ALU.mult).then_inc(g["y"], 1)
                    else:
                        dve.wait_ge(g["o_hi"], hd + 1)
                        nc.vector.tensor_tensor(xL[:, 4 + hd, :], oy, xH[:, 4 + hd, :].bitcast(F32), ALU.subtract)\
                            .then_inc(g["o_lo"], 1)

                def select(n):
                    u, l = n // LEVELS, n % LEVELS
                    hd, d = head_dir(u)
                    dve.wait_ge(g["level"], n + 1)
                    dve.wait_ge(g["diag_out"], hd + 1)
                    if n:
                        dve.wait_ge(g["pred"], n)
                    nc.vector.copy_predicated(aT[:, hd % 2, :, :], level_mask[:, d, l * P:(l + 1) * P].unsqueeze(1).to_broadcast([P, NB, P]),
                                              bank[n % 3][:, :].rearrange("s (c t) -> s c t", c=NB)).then_inc(g["pred"], 1)

                for n in range(JOBS + LAG):
                    if n < JOBS:
                        u, l = n // LEVELS, n % LEVELS
                        hd, d = head_dir(u)
                        if n >= 4:
                            dve.wait_ge(g["mult"], n - 3)
                        q, k, border = halves(bx(u), u, l)
                        dq, dk, _ = halves(dec[:, n % 4, :], u, l)
                        nc.vector.tensor_tensor(dq, q, border, ALU.subtract)
                        nc.vector.tensor_tensor(dk, border, k, ALU.subtract).then_inc(g["diff"], 1)
                        if l == 6:
                            states(u)
                        if (u, l) in vector_reads:
                            read_out(*vector_reads[u, l])
                    if n >= LAG:
                        select(n - LAG)
                read_out(HG - 1, 0)
                read_out(HG - 1, 1)

            @block.tensor
            def _(pe):
                for hd in range(HG):
                    if hd:
                        pe.wait_ge(g["v_out"], 2 * hd)
                    for c in range(NB):
                        mm = nc.tensor.transpose(bank[3][:, blk(c)], sb_hT[:, SB_I + hd, blk(c)], ident[:, :])
                    mm.then_inc(g["v_turned"], 1)
                    for c in range(2):
                        mm = nc.tensor.transpose(bank[4][:, blk(c)], sb_hc[:, SB_I - SB_CTX + hd, blk(c)], ident[:, :])
                    mm.then_inc(g["v_turned"], 1)
                pe.wait_ge(g["v_out"], 2 * HG)

                def turn(u):
                    pe.wait_ge(g["kd"], u + 1)
                    if u:
                        pe.wait_ge(g["kd_out"], u)
                    for p in range(3):
                        nc.tensor.transpose(bank[3][:, blk(p)], kds[u % 2][:, blk(p)], ident[:, :])
                    for p in range(2):
                        mm = nc.tensor.transpose(bank[4][:, blk(p)], kds[u % 2][:, blk(3 + p)], ident[:, :])
                    mm.then_inc(g["kd_turned"], 1)

                def sums(u):
                    hd, d = head_dir(u)
                    pe.wait_ge(g["kd_out"], u + 1)
                    if u:
                        pe.wait_ge(g["state"], 4 * u)
                    for c in range(2):
                        nc.tensor.matmul(bank[5][:, 0:P], kd_tm[:, 3 + c, :], v_tm7[:, hd, NB + c, :], start=c == 0, stop=c == 1)
                    for p in range(3):
                        c = chunk_at(u, p)
                        mm = nc.tensor.matmul(bank[5][:, blk(p + 1)], kd_tm[:, c - d, :], v_tm7[:, hd, c, :], start=True, stop=True)
                    mm.then_inc(g["kv"], 1)

                def diagonal(hd):
                    pe.wait_ge(g["ksum"], hd + 1)
                    if hd == 1:
                        pe.wait_ge(g["diag_out"], 1)
                    elif hd:
                        pe.wait_ge(g["rstd"], 2 * hd - 3)
                    for c in range(NB):
                        mm = nc.tensor.matmul(bank[7][:, blk(c)], ksum[:, blk(c)], sb_hT[:, SB_HQ + hd, blk(c)],
                                              start=True, stop=True)
                    mm.then_inc(g["diag"], 1)

                def output(hd):
                    pe.wait_ge(g["pred"], 2 * LEVELS * (hd + 1))
                    pe.wait_ge(g["state"], 8 * (hd + 1))
                    pe.wait_ge(g["qe"], 2 * (hd + 1))
                    if hd:
                        pe.wait_ge(g["y"], 2 * hd)
                    for c in range(NB):
                        o = bank[6][:, blk(c)]
                        nc.tensor.matmul(o, v_tm7[:, hd, c, :], aT[:, hd % 2, c, :], start=True, stop=False)
                        for d in range(2):
                            u = 2 * hd + d
                            mm = nc.tensor.matmul(o, state[:, u % 4, chunk_at(u, c), :], qe[:, u % 4, blk(c)],
                                                  start=False, stop=d == 1)
                    mm.then_inc(g["o"], 1)

                def mean(hd):
                    pe.wait_ge(g["sq"], hd + 1)
                    pe.wait_ge(g["diag_out"], min(hd + 2, HG))
                    nc.tensor.matmul(bank[7][:, :], mean_of[:, :], osq, start=True, stop=True).then_inc(g["mean"], 1)

                turn(0)
                diagonal(0)
                for n in range(JOBS):
                    u, l = n // LEVELS, n % LEVELS
                    hd, d = head_dir(u)
                    pe.wait_ge(g["mult"], n + 1)
                    if n >= 3:
                        pe.wait_ge(g["pred"], n - 2)
                    x = mixed[:, n % 4, :]
                    for c in range(NB):
                        mm = nc.tensor.matmul(bank[n % 3][:, blk(c)], x[:, blk(c)], x[:, blk(c)], start=True, stop=True)
                    mm.then_inc(g["level"], 1)
                    if l == 2:
                        sums(u)
                    if l == 3 and d == 0 and hd:
                        output(hd - 1)
                    if l == 4 and u + 1 < U7:
                        turn(u + 1)
                    if l == 6 and d == 0 and hd:
                        mean(hd - 1)
                    if l == 6 and d == 1 and hd + 1 < HG:
                        diagonal(hd + 1)
                output(HG - 1)
                mean(HG - 1)

        stages = [Residual(W["sb_out"], X, 1, gate=16)]
        f0 = stages[0].f0
        stages.append(Norm("rms", xT, lambda t: gmod[:, 1, t:t + 1], lambda t: modT[:, 24 + t, 0:1], 1, X,
                           (x_ready, take("x_ready", KD)), source=lambda t: (acc_free[t % 2], f0[t % 2] + t // 2 + 2)))
        stages.append(Up(W["up2"], stages[-1].ready[1]))
        stages.append(Residual(W["down2"], (hidH, hidL), 2, gate=40, hidden=stages[-1].done))
        f1 = stages[-1].f0
        stages.append(Norm("final", xT, param("gf"), None, 1, source=lambda t: (acc_free[1], f1[1] + KD // 2 + 1)))
        stages.append(Store(stages[-1]))
        run(stages)

def t5_bucket(dist):
    half = N_BUCKETS // 2
    n = np.maximum(dist, 0)
    nf = np.maximum(n, 1).astype(np.float32)
    large = half + (np.log(nf / np.float32(half)) / np.float32(math.log(T5_MAX / half)) * np.float32(N_BUCKETS - half)).astype(np.int32)
    return np.where(n < half, n, np.minimum(large, N_BUCKETS - 1))


def rope_constants():
    half, axis = HD // 4, HD // 2
    turn = np.zeros((HD, HD), np.float32)
    for ax in range(2):
        for d in range(half):
            turn[ax * axis + d, ax * axis + half + d] = -1.0
            turn[ax * axis + half + d, ax * axis + d] = 1.0
    n_rows = T // GRID_W
    row = np.repeat(np.arange(n_rows, dtype=np.float32), GRID_W)
    column = np.tile(np.arange(GRID_W, dtype=np.float32), n_rows)
    inv = np.float32(ROPE_THETA) ** (-np.arange(0, axis, 2, dtype=np.float32) / np.float32(axis))
    ar, ac = row[:, None] * inv, column[:, None] * inv
    ang = np.concatenate([ar, ar, ac, ac], axis=-1).T
    c, s = np.tile(np.cos(ang), (2, 1)), np.tile(np.sin(ang), (2, 1))
    scale = np.float32(HD ** -0.5)
    return np.kron(np.eye(2), turn).T, np.stack([c * scale, s * scale, c, s], axis=1)


def level_masks():
    t = np.arange(P)
    m = []
    for l in range(P.bit_length() - 1):
        h = P >> (l + 1)
        same, upper = t[:, None] // (2 * h) == t[None, :] // (2 * h), t // h % 2 == 1
        m.append(same & ~upper[:, None] & upper[None, :])
    m = np.stack(m)
    return np.stack([m, m.swapaxes(1, 2)]).transpose(0, 2, 1, 3).reshape(2, P, -1)


def layout(i):
    def chunked(w):
        k, n = w.shape
        return w.reshape(k // P, P, n // P, P).transpose(2, 1, 0, 3).reshape(n // P, P, k)

    def halves(w):
        k, n = w.shape
        return w.reshape(2, k // P // 2, P, n // P, P).transpose(3, 0, 2, 1, 4).reshape(2 * n // P, P, k // 2)

    def pairs(w):
        c = chunked(w)
        return c.reshape(2, c.shape[0] // 2, *c.shape[1:]).swapaxes(0, 1).reshape(c.shape)

    def col(v):
        return v.reshape(-1, P).T

    def parts(w, widths):
        return np.split(w, np.cumsum(widths)[:-1], axis=1)

    a = {}
    a["xT"] = i["x"][0].T.reshape(KD, P, T).transpose(1, 0, 2)
    qa, ckv, qi, ki, wi, qb, kb, vb, fi = parts(i["ev_w_in"][0], (512, P, 512, HD, HEADS, 512, 512, 512, HEADS))
    misc = np.zeros((D, P), np.float32)
    misc[:, 0:HEADS] = fi
    misc[:, W_IDX_ROW:W_IDX_ROW + HEADS] = wi
    a["ev_in"] = chunked(np.concatenate([qa, qi, qb, kb, vb, ckv, ki, ki, misc], axis=1))
    a["mod"] = i["w_mod_2"][0].T.reshape(-1, P, D)
    a["ev_out"] = chunked(i["ev_w_o"][0])
    a["od_in"] = chunked(i["od_w_in"][0])
    a["od_out"] = chunked(i["od_w_o"][0])
    q, k, v, hq, hi, ff, fb, hg = parts(i["w_in_2"][0], (512, P, P, 512, 512, 512, 512, 512))
    q = q.reshape(D, 2, 4, HD).swapaxes(1, 2).reshape(D, 512)
    a["sb_in"] = chunked(np.concatenate([q, hq, hg, k, v, hi, ff, fb], axis=1))
    wo = i["w_out_2"][0]
    a["sb_out"] = chunked(np.concatenate([wo[0:512].reshape(2, 4, HD, D).swapaxes(0, 1).reshape(512, D), wo[512:]]))
    for n in range(2):
        a[f"up{n}"] = pairs(i["ffn_w_up"][n])
        a[f"down{n}"] = halves(i["ffn_w_down"][n])
    a["up2"] = pairs(i["w_gu_2"][0])
    a["down2"] = halves(i["w_down_2"][0])
    a["ident"] = np.eye(P, dtype=np.float32)
    a["mean_of"] = np.full((P, P), 1.0 / D, np.float32)
    a["rel_bias"] = i["rel_bias"]
    dist = 2 * P - 1 - np.arange(SKEW)
    a["onehot"] = (t5_bucket(dist)[None, :] == np.arange(N_BUCKETS)[:, None]).astype(np.float32)
    a["c_rows"] = np.tile(np.stack([i["c_2"][0], i["c_ctx_2"]])[:, None, :], (1, P, 1))
    a["w_uk"] = i["ev_w_uk"][0].transpose(0, 2, 1).reshape(4, P, P).transpose(1, 0, 2)
    a["w_uv"] = i["ev_w_uv"][0].transpose(1, 0, 2)

    a["sgu_w"] = i["od_sgu_w"][0].transpose(2, 0, 1)
    a["sgu_b"] = i["od_sgu_b"][0].reshape(4, 2, 1, P).repeat(HD, axis=2).reshape(4, P, P).transpose(1, 0, 2)
    a["sgu_g"] = np.tile(i["od_sgu_g"][0].reshape(1, -1), (P, 1))
    a["cT"] = i["ctx_2"][0].T.reshape(KD, P, LC).transpose(1, 0, 2)
    a["mean64"] = np.kron(np.eye(2), np.full((HD, HD), 1.0 / HD))
    a["turn64"], a["rope"] = rope_constants()
    put, n = {}, 0
    a["level_masks"] = level_masks()
    parts_ = []
    def column(name, v):
        nonlocal n
        put[name] = n
        parts_.append(v)
        n += v.shape[1]
    bf = np.zeros((P, 1), np.float32)
    bf[0:HEADS, 0] = i["ev_b_f"][0]
    column("b_f", bf)
    column("eps", np.tile(np.array([[LN_EPS, RMS_EPS]], np.float32), (P, 1)))
    column("b_mod", col(i["b_mod_2"][0]))
    for l in range(2):
        for s in range(2):
            column(f"ln_g{l}{s}", col(i["ln_g"][l, s]))
            column(f"ln_b{l}{s}", col(i["ln_b"][l, s]))
        c = pairs_conv(i["ffn_conv_w"][l])
        column(f"conv{l}", c)
    column("od_conv", i["od_conv_w"][0].T.reshape(4, P, 3).transpose(1, 0, 2).reshape(P, 12))
    column("g1", col(i["g_norm1_2"][0]))
    column("g2", col(i["g_norm2_2"][0]))
    column("gf", col(i["g_final_2"]))
    column("g_q", np.tile(i["g_q_2"][0], 2)[:, None])
    column("g_k", np.tile(i["g_k_2"][0], 2)[:, None])
    column("g_hg", i["g_hg_2"][0][:, None])
    column("lb_raw", i["lb_raw_2"].reshape(2 * 2 * HG, P).T)
    a["cols"] = np.concatenate(parts_, axis=1)
    return {n_: np.ascontiguousarray(v_, dtype=np.float32) for n_, v_ in a.items()}, put


def pairs_conv(w):
    c = w.T.reshape(2, NFF, P, 3).transpose(2, 1, 0, 3)
    return c.reshape(P, 2 * NFF * 3)


def kernel(**inputs):
    import concourse.bacc as _bacc
    from concourse.bass_utils import run_bass_kernel_spmd as _run

    nc = _bacc.Bacc("TRN2", target_bir_lowering=False, num_devices=1)
    arrays, place = layout({n: np.asarray(v) for n, v in inputs.items()})
    A = {n: nc.dram_tensor(f"in_{n}", v.shape, mybir.dt.from_np(v.dtype), kind="ExternalInput").ap()
         for n, v in arrays.items()}
    A["place"] = place
    out = nc.dram_tensor("out", (P, KD, T), F32, kind="ExternalOutput").ap()
    build(nc, A, out)
    r = _run(nc, [{f"in_{n}": v for n, v in arrays.items()}], core_ids=[0])
    return np.ascontiguousarray(r.results[0]["out"].transpose(2, 1, 0).reshape(1, T, D))
```
